# Optimizing a Trainium2 kernel written in Bass

```python
import math
import jax, jax.numpy as jnp
from jax import lax
import numpy as np

D_MODEL = 1024
BATCH = 1
SEQ = 1024
DEPTH = 1

CHUNK = 64
HEAD_DIM = 64
D_MIX = D_MODEL
ROPE_THETA = 10000.0
NORM_EPS = 1e-6
SUBLN_EPS = 1e-5
NEG_INF = -1e30
SWA_WIDTH = D_MIX // 2
SWA_HEADS = SWA_WIDTH // HEAD_DIM
SWA_KV_HEADS = 2
SWA_GROUP = SWA_HEADS // SWA_KV_HEADS
SWA_WINDOW = 128
SWA_WINDOW_CHUNKS = SWA_WINDOW // CHUNK
DIFF_WIDTH = D_MIX - SWA_WIDTH
DIFF_HEADS = DIFF_WIDTH // (2 * HEAD_DIM)
Q_BLOCK = 128
Q_A = SWA_HEADS * HEAD_DIM
K_A = SWA_KV_HEADS * HEAD_DIM
V_A = SWA_KV_HEADS * HEAD_DIM
G_A = SWA_WIDTH
Q_B = DIFF_HEADS * 2 * HEAD_DIM
K_B = DIFF_HEADS * 2 * HEAD_DIM
V_B = DIFF_HEADS * 2 * HEAD_DIM
G_B = DIFF_WIDTH
IN_COLS = [Q_A, K_A, V_A, G_A, Q_B, K_B, V_B, G_B]
SPLITS = [int(v) for v in np.cumsum(IN_COLS)[:-1]]
D_IN = int(sum(IN_COLS))

kernel_name = "hymba_swa_sink_diffattn_gated_trunk"

def rmsnorm(x, w, eps):
    xf = x.astype(jnp.float32)
    y = xf * lax.rsqrt(jnp.mean(xf * xf, axis=-1, keepdims=True) + eps)
    return y.astype(x.dtype) * w

def rope_tables(seq, dim):
    inv_freq = 1.0 / (ROPE_THETA ** (jnp.arange(0, dim, 2, dtype=jnp.float32) / dim))
    pos = jnp.arange(seq, dtype=jnp.float32)
    freqs = pos[:, None] * inv_freq[None, :]
    emb = jnp.concatenate([freqs, freqs], axis=-1)
    return jnp.cos(emb), jnp.sin(emb)

def apply_rope(x, cos, sin):
    shape = (cos.shape[0],) + (1,) * (x.ndim - 3) + (cos.shape[1],)
    c, s = cos.reshape(shape), sin.reshape(shape)
    xf = x.astype(jnp.float32)
    x1, x2 = jnp.split(xf, 2, axis=-1)
    rot = jnp.concatenate([-x2, x1], axis=-1)
    return (xf * c + rot * s).astype(x.dtype)

def chunk_band(t, n_chunks):
    parts = []
    for j in range(n_chunks - 1, 0, -1):
        parts.append(jnp.pad(t, ((0, 0), (j, 0), (0, 0), (0, 0), (0, 0)))[:, :-j])
    parts.append(t)
    return jnp.concatenate(parts, axis=2)

def sliding_window_sink_attention(q, k, v, sinks):
    B, S, _, Dh = q.shape
    nc = S // CHUNK
    qc = q.reshape(B, nc, CHUNK, SWA_KV_HEADS, SWA_GROUP, Dh)
    kb = chunk_band(k.reshape(B, nc, CHUNK, SWA_KV_HEADS, Dh), SWA_WINDOW_CHUNKS)
    vb = chunk_band(v.reshape(B, nc, CHUNK, SWA_KV_HEADS, Dh), SWA_WINDOW_CHUNKS)
    s = jnp.einsum('bnqhgd,bnkhd->bnhgqk', qc, kb).astype(jnp.float32) * (Dh ** -0.5)
    band = SWA_WINDOW_CHUNKS * CHUNK
    offset = SWA_WINDOW_CHUNKS - 1 - jnp.arange(band) // CHUNK
    valid = jnp.arange(nc)[:, None] >= offset[None, :]
    s = jnp.where(valid[None, :, None, None, None, :], s, NEG_INF)
    sink = sinks.astype(jnp.float32).reshape(1, 1, SWA_KV_HEADS, SWA_GROUP, 1, 1)
    sink = jnp.broadcast_to(sink, s.shape[:-1] + (1,))
    p = jax.nn.softmax(jnp.concatenate([s, sink], axis=-1), axis=-1)[..., :-1]
    o = jnp.einsum('bnhgqk,bnkhd->bnqhgd', p.astype(v.dtype), vb)
    return o.reshape(B, S, SWA_HEADS * Dh)

def differential_attention(q, k, v, lam, subln_w, lambda_init):
    B, S, H, _, Dh = q.shape
    nb = S // Q_BLOCK
    qb = jnp.moveaxis(q.reshape(B, nb, Q_BLOCK, H, 2, Dh), 1, 0)
    key_chunk = jnp.arange(S) // CHUNK
    scale = Dh ** -0.5

    def block(args):
        i, qi = args
        q_chunk = (i * Q_BLOCK + jnp.arange(Q_BLOCK)) // CHUNK
        allowed = key_chunk[None, :] <= q_chunk[:, None]
        s = jnp.einsum('bqhtd,bkhtd->bhtqk', qi, k).astype(jnp.float32) * scale
        p = jax.nn.softmax(jnp.where(allowed, s, NEG_INF), axis=-1)
        a = p[:, :, 0] - lam * p[:, :, 1]
        return jnp.einsum('bhqk,bkhe->bqhe', a.astype(v.dtype), v)

    out = lax.map(block, (jnp.arange(nb), qb))
    out = jnp.moveaxis(out, 0, 1).reshape(B, S, H, 2 * Dh)
    out = rmsnorm(out, subln_w, SUBLN_EPS) * (1.0 - lambda_init)
    return out.reshape(B, S, H * 2 * Dh)

def setup_inputs(seed: int = 0) -> dict:
    key = jax.random.key(seed)
    ks = jax.random.split(key, 12)
    f32 = jnp.float32
    x = jax.random.normal(ks[0], (BATCH, SEQ, D_MODEL), f32)
    norm_w = 1.0 + 0.02 * jax.random.normal(ks[1], (DEPTH, D_MODEL), f32)
    w_in = jax.random.normal(ks[2], (DEPTH, D_MODEL, D_IN), f32) * D_MODEL ** -0.5
    sinks = 0.5 * jax.random.normal(ks[3], (DEPTH, SWA_HEADS), f32)
    lambda_q1 = 0.1 * jax.random.normal(ks[4], (DEPTH, HEAD_DIM), f32)
    lambda_k1 = 0.1 * jax.random.normal(ks[5], (DEPTH, HEAD_DIM), f32)
    lambda_q2 = 0.1 * jax.random.normal(ks[6], (DEPTH, HEAD_DIM), f32)
    lambda_k2 = 0.1 * jax.random.normal(ks[7], (DEPTH, HEAD_DIM), f32)
    subln_w = 1.0 + 0.02 * jax.random.normal(ks[8], (DEPTH, 2 * HEAD_DIM), f32)
    w_o = jax.random.normal(ks[9], (DEPTH, D_MIX, D_MODEL), f32) * D_MIX ** -0.5
    final_norm_w = 1.0 + 0.02 * jax.random.normal(ks[10], (D_MODEL,), f32)
    return {"x": x, "norm_w": norm_w, "w_in": w_in, "sinks": sinks,
            "lambda_q1": lambda_q1, "lambda_k1": lambda_k1,
            "lambda_q2": lambda_q2, "lambda_k2": lambda_k2,
            "subln_w": subln_w, "w_o": w_o, "final_norm_w": final_norm_w}

def reference(x, norm_w, w_in, sinks, lambda_q1, lambda_k1, lambda_q2, lambda_k2,
              subln_w, w_o, final_norm_w):
    B, S, _ = x.shape
    cos, sin = rope_tables(S, HEAD_DIM)
    for l in range(DEPTH):
        lambda_init = 0.8 - 0.6 * math.exp(-0.3 * l)
        h = rmsnorm(x, norm_w[l], NORM_EPS)
        proj = jnp.einsum('bsd,de->bse', h, w_in[l])
        q_a, k_a, v_a, g_a, q_b, k_b, v_b, g_b = jnp.split(proj, SPLITS, axis=-1)
        q_a = apply_rope(q_a.reshape(B, S, SWA_HEADS, HEAD_DIM), cos, sin)
        k_a = apply_rope(k_a.reshape(B, S, SWA_KV_HEADS, HEAD_DIM), cos, sin)
        v_a = v_a.reshape(B, S, SWA_KV_HEADS, HEAD_DIM)
        out_a = sliding_window_sink_attention(q_a, k_a, v_a, sinks[l]) * jax.nn.silu(g_a)
        q_b = apply_rope(q_b.reshape(B, S, DIFF_HEADS, 2, HEAD_DIM), cos, sin)
        k_b = apply_rope(k_b.reshape(B, S, DIFF_HEADS, 2, HEAD_DIM), cos, sin)
        v_b = v_b.reshape(B, S, DIFF_HEADS, 2 * HEAD_DIM)
        lam = (jnp.exp(jnp.sum(lambda_q1[l].astype(jnp.float32) * lambda_k1[l].astype(jnp.float32)))
               - jnp.exp(jnp.sum(lambda_q2[l].astype(jnp.float32) * lambda_k2[l].astype(jnp.float32)))
               + lambda_init)
        out_b = differential_attention(q_b, k_b, v_b, lam, subln_w[l], lambda_init) * jax.nn.silu(g_b)
        mix = jnp.concatenate([out_a, out_b], axis=-1)
        x = x + jnp.einsum('bse,ed->bsd', mix, w_o[l])
    return rmsnorm(x, final_norm_w, NORM_EPS)


_drawn_inputs = setup_inputs


def setup_inputs(seed=0):
    import zlib

    import numpy as np

    out = dict(_drawn_inputs(seed))
    spreads = {}
    factors = {'norm_w': 3.843,
     'sinks': 64.0,
     'lambda_k1': 5.688,
     'lambda_q2': 6.038,
     'subln_w': 25.096,
     'final_norm_w': 8.493}
    for name, (base, spread) in spreads.items():
        noise = np.random.default_rng([zlib.crc32(name.encode()), seed]).standard_normal(out[name].shape)
        drawn = base * np.exp(spread * noise) if base else spread * noise
        out[name] = __import__('jax').numpy.asarray(drawn.astype(out[name].dtype))
    for name, factor in factors.items():
        out[name] = (out[name] * factor).astype(out[name].dtype)
    return out
```

```python
from contextlib import ExitStack

import numpy as np

import concourse.bass as bass
from concourse import mybir

F32 = mybir.dt.float32
F32R = mybir.dt.float32r
ALU = mybir.AluOpType
ACT = mybir.ActivationFunctionType
AX_X = mybir.AxisListType.X

P = 128
S = 1024
D = 1024
HD = 64
KD = D // P
NS = S // P
HALF = 512
NEG = -1e30
CHUNK = 64
NB = 4
SCALE = HD ** -0.5
LAMBDA_INIT = 0.8 - 0.6
NORM_EPS = 1e-6
SUBLN_EPS = 1e-5
QA, KA, VA, GA, QB, KB, VB, GB = 0, 512, 640, 768, 1280, 1792, 2304, 2816


def weight_tiles():
    tiles = []
    for h in range(NB):
        tiles += [("kb", h), ("qb", h), ("vb", h)]
    tiles += [("ka", 0), ("va", 0)] + [("qa", t) for t in range(4)]
    tiles += [("gb", h) for h in range(NB)] + [("ga", t) for t in range(4)]
    return tiles


TILES = weight_tiles()
NT = len(TILES)
PROLOGUE = 6
WA = NB * NS
COLUMNS = {"qa": QA, "ka": KA, "va": VA, "ga": GA, "qb": QB, "kb": KB, "vb": VB, "gb": GB}


def make_plan():
    plan = [("split", 0), ("xnorm", 0)]
    for s in range(NS):
        plan += [("xnorm", s + 1)] if s + 1 < NS else []
        plan += [("xturn", s)]
        plan += [("split", 1)] if s == 1 else []
        plan += [("proj", (0, 0), 0, 24), ("copy", (0, 0))] if s == NS // 2 - 1 else []
    halves = [(n, h) for n in range(NT) for h in range(2)]
    for j in range(1, PROLOGUE):
        n, h = halves[j]
        plan += [("split", n + 1)] if h == 0 else []
        plan += [("proj", (n, h), 0, 24), ("copy", (n, h)), ("place", halves[j - 1])]
    plan += [("scores", 0, 0), ("scores", 0, 1), ("softmax", 0), ("place", halves[PROLOGUE - 1])]
    rest = halves[PROLOGUE:]
    before = None
    for w in range(WA + 2 * NS):
        take = w < WA - 2 or (w >= WA and w % 2 == 0)
        fill = rest.pop(0) if take else None
        plan += [("split", fill[0] + 1)] if fill and fill[1] == 0 else []
        plan += [("proj", fill, 0, 12)] if fill else []
        if w + 1 < WA + 2 * NS:
            plan += [("scores", w + 1, m) for m in range(2) if w + 1 < WA or m == (w + 1) % 2]
        plan += [("turns", w)]
        plan += [("proj", fill, 12, 24)] if fill else []
        plan += [("softmax", w + 1)] if w + 1 < WA + 2 * NS else []
        plan += [("copy", fill)] if fill else []
        plan += [("values", w)]
        plan += [("place", before)] if before else []
        before = fill
    plan += [("place", before)] if before else []
    before = None
    for n, h in rest:
        plan += [("split", n + 1)] if h == 0 and n + 1 < NT else []
        plan += [("proj", (n, h), 0, 24), ("copy", (n, h))]
        plan += [("place", before)] if before else []
        before = (n, h)
    plan += [("split", NT + e) for e in range(KD)]
    plan += [("place", before), ("msplit", 0), ("msplit", 1)]
    for i in range(NS):
        plan += [("out", i), ("result", i)]
        plan += [("msplit", i + 2)] if i + 2 < NS else []
    return plan


PLAN = make_plan()


def build(nc, x, norm_w, w_in, sinks, lq1, lk1, lq2, lk2, subln_w, w_o, final_w, cos_t, sin_t, out):
    x_rows = x.rearrange("b (i p) d -> p (b i) d", p=P)
    out_rows = out.rearrange("b (i p) d -> p (b i) d", p=P)
    w_cols = w_in.rearrange("l (k p) c -> p (l k) c", p=P)

    with ExitStack() as ctx:
        def keep(name, shape, dt=F32):
            return ctx.enter_context(nc.sbuf_tensor(name, shape, dt))

        ident = keep("ident", [P, P])
        w_raw = keep("w_raw", [P, 2, KD, P])
        w_hi = keep("w_hi", [P, 2, KD, P], F32R)
        w_lo = keep("w_lo", [P, 2, KD, P], F32R)
        o_b = keep("o_b", [P, NB, NS, P])
        raw = keep("raw", [P, 2, HALF])
        swp = keep("swp", [P, 2, HALF])
        o_sq = keep("o_sq", [P, 4, P])
        minus_half = keep("minus_half", [P, 8])
        ss = keep("ss", [P, 6, 8])
        ms = keep("ms", [P, 6, 8])
        rstd = keep("rstd", [P, 6, 8])
        lam_in = keep("lam_in", [P, 4, HD])
        lam_s = keep("lam_s", [P, 8])
        lam_junk = keep("lam_junk", [P, 2, HD])
        neg_lam = keep("neg_lam", [P, 1])
        sub_w = keep("sub_w", [P, 1])
        sub_ws = keep("sub_ws", [P, 1])
        sink = keep("sink", [P, 8])
        neg_sink = keep("neg_sink", [P, 8])
        nmax = keep("nmax", [P, 2, 4])
        rsum = keep("rsum", [P, 2, 4])
        rinv = keep("rinv", [P, 2, 4])
        esink = keep("esink", [P, 2, 4])
        with ExitStack() as early:
            def first(name, shape, dt=F32):
                return early.enter_context(nc.sbuf_tensor(name, shape, dt))

            qb = first("qb", [P, 2, S])
            kb = first("kb", [P, 2, 2, S])
            vb = first("vb", [P, 2, NS, P])
            qa = first("qa", [P, 4, S])
            ka = first("ka", [P, 2, S])
            va = first("va", [P, NS, P])
            pr = first("pr", [P, 2, S])
            at = first("at", [P, 2, S])
            aT = first("aT", [P, 2, HALF])
            cos = first("cos", [P, S])
            sin = first("sin", [P, S])
            xT_hi = first("xT_hi", [P, KD, S], F32R)
            xT_lo = first("xT_lo", [P, KD, S], F32R)
        with ExitStack() as tail:
            def last_of(name, shape, dt=F32):
                return tail.enter_context(nc.sbuf_tensor(name, shape, dt))

            mixA = last_of("mixA", [P, 4, S])
            wo_hi = last_of("wo_hi", [P, KD, D], F32R)
            wo_lo = last_of("wo_lo", [P, KD, D], F32R)
            fin_w = last_of("fin_w", [P, D])
            unused = last_of("unused", [P, D])
            mix_hi = last_of("mix_hi", [P, 2, KD, P], F32R)
            mix_lo = last_of("mix_lo", [P, 2, KD, P], F32R)
            x_again = last_of("x_again", [P, 2, D])
            y = last_of("y", [P, 2, D])
            res = last_of("res", [P, 2, D])
        x_in = o_b[:].rearrange("p h i e -> p (h i e)").rearrange("p (b d) -> p b d", d=D)
        mixB = o_b[:].rearrange("p h i e -> p h (i e)")
        norm_row = at[:, 1, :]
        at_a = at[:].rearrange("p b (h k) -> p b h k", h=4)
        pr_a = pr[:].rearrange("p b (h k) -> p b h k", h=4)

        def psum(name, shape):
            return ctx.enter_context(nc.psum_tensor(name, shape, F32))

        pS = psum("pS", [P, 2, 1024])
        pT = psum("pT", [P, 2, HALF])
        pO = psum("pO", [P, HALF])
        pP = psum("pP", [P, HALF])
        pS_a = pS[:].rearrange("p b (h k) -> p b h k", h=4)

        def sem(name):
            return ctx.enter_context(nc.semaphore(name))

        const_in = sem("const_in")
        norm_in = sem("norm_in")
        table_in = sem("table_in")
        x_in_s = [sem(f"x_in{b}") for b in range(4)]
        const_ok = sem("const_ok")
        lam_dot = sem("lam_dot")
        lam_exp = sem("lam_exp")
        x_ss = sem("x_ss")
        x_rstd = sem("x_rstd")
        x_norm = sem("x_norm")
        turn_ok = sem("turn_ok")
        turn_act = sem("turn_act")
        turn_dve = sem("turn_dve")
        xhi_ok = sem("xhi_ok")
        w_in_s = [sem(f"w_in{b}") for b in range(2)]
        w_hi_ok = sem("w_hi_ok")
        w_lo_ok = sem("w_lo_ok")
        proj_ok = sem("proj_ok")
        copy_ok = sem("copy_ok")
        gate_ok = sem("gate_ok")
        swap_s = [sem(f"swap{b}") for b in range(2)]
        rope_mul = sem("rope_mul")
        rope_ok = sem("rope_ok")
        scores_ok = [sem(f"scores_ok{m}") for m in range(2)]
        max_ok = [sem(f"max_ok{m}") for m in range(2)]
        exp_ok = [sem(f"exp_ok{m}") for m in range(2)]
        esink_ok = sem("esink_ok")
        at_ok = sem("at_ok")
        av_ok = sem("av_ok")
        o_copied = sem("o_copied")
        o_ss = sem("o_ss")
        o_rstd = sem("o_rstd")
        o_norm = sem("o_norm")
        mixa_ok = sem("mixa_ok")
        mhi_ok = sem("mhi_ok")
        mlo_ok = sem("mlo_ok")
        out_ok = sem("out_ok")
        y_ok = sem("y_ok")
        y_ss = sem("y_ss")
        y_rstd = sem("y_rstd")
        res_ok = sem("res_ok")
        x_again_s = [sem(f"x_again{b}") for b in range(2)]
        fin_in = sem("fin_in")
        stored = [sem(f"stored{b}") for b in range(2)]
        dve_chain = sem("dve_chain")
        pool_chain = sem("pool_chain")

        projs = [st[1] for st in PLAN if st[0] == "copy"]
        kind_of = [TILES[t][0] for t, _ in projs]
        number = {ph: n for n, ph in enumerate(projs)}
        n_attention = max(n for n, ph in enumerate(projs) if PLAN.index(("copy", ph)) < PLAN.index(("values", WA + 2 * NS - 1)))

        def count(n, kinds):
            return sum(k in kinds for k in kind_of[:n])

        ROTARY, VALUE, GATE = ("qa", "ka", "qb", "kb"), ("va", "vb"), ("ga", "gb")

        def bank_no(n):
            return n % 4 if n < PROLOGUE or n > n_attention else 4

        def bank(n):
            b = bank_no(n)
            return pP[:, :] if b == 4 else pS[:, b // 2, (b % 2) * HALF:(b % 2 + 1) * HALF]

        turns = []
        for st in PLAN:
            if st[0] == "xturn":
                turns += [("x", st[1], r) for r in range(2)]
            if st[0] == "place" and TILES[st[1][0]][0] in VALUE:
                turns.append(("v", st[1]))
            if st[0] == "place" and TILES[st[1][0]][0] == "gb":
                turns.append(("o", st[1]))
            if st[0] == "turns":
                w = st[1]
                n_turns = (w % NS + 4) // 4 if w < WA else (1 if w < WA + 2 else 2)
                turns += [("a", w, r) for r in range(n_turns)]
        turn_no = {t: n for n, t in enumerate(turns)}
        att_turns = [t for t in turns if t[0] == "a"]
        att_no = {t: n for n, t in enumerate(att_turns)}

        def turns_of(w):
            return [t for t in att_turns if t[1] == w]

        def turns_read(n, kinds):
            return sum(t[0] in kinds for t in turns[:n + 1])

        def wait_bank_free(pe, n):
            earlier = [j for j in range(n) if bank_no(j) == bank_no(n)]
            if earlier:
                pe.wait_ge(copy_ok, earlier[-1] + 1)
                if kind_of[earlier[-1]] in GATE:
                    pe.wait_ge(gate_ok, count(earlier[-1] + 1, GATE))
            if n > n_attention:
                pe.wait_ge(exp_ok[bank_no(n) // 2], WA + NS)

        def wait_stage_free(eng, n):
            if n < 2:
                return
            if kind_of[n - 2] == "gb":
                eng.wait_ge(turn_dve, turns_read(turn_no[("o", projs[n - 2])], ("x", "o")))
            elif kind_of[n - 2] == "ga":
                eng.wait_ge(mixa_ok, count(n - 1, ("ga",)))
            elif kind_of[n - 2] in VALUE:
                eng.wait_ge(turn_ok, turn_no[("v", projs[n - 2])] + 1)
            else:
                eng.wait_ge(rope_ok, count(n - 1, ROTARY))

        def swaps(n):
            return 64 * sum(kind_of[j] in ROTARY for j in range(n % 2, n + 1, 2))

        def tile_done(kind, j, half=1):
            return number[(TILES.index((kind, j)), half)] + 1

        def o_visit(w):
            return w // 4 if w < WA else NS + w - WA

        def visit(w):
            return w if w < WA else WA + (w - WA) // 2

        def o_stat(stat, v):
            return stat[:, 2 + v // 2, 4 * (v % 2):4 * (v % 2) + 4]

        def columns_a(i):
            return (P, P) if i == 0 else (CHUNK, P + CHUNK)

        block = ctx.enter_context(nc.Block())

        @block.sync
        def _(sp):
            def load_w(n):
                if n >= NT + KD:
                    return
                if n >= 2:
                    sp.wait_ge(w_hi_ok, n - 1)
                    sp.wait_ge(w_lo_ok, n - 1)
                b = n % 2
                if n >= NT:
                    e = n - NT
                    dst = w_raw[:, b].rearrange("p k c -> p (k c)")
                    for g in range(2):
                        r = g * 4 * HD + e * HD if e < 4 else e * P + g * HD
                        sp.dma_start(dst[g * HD:(g + 1) * HD], w_o[0, r:r + HD, :]).then_inc(w_in_s[b], 16)
                    return
                kind, j = TILES[n]
                for g in range(2):
                    if kind in ("qa", "ga"):
                        c = COLUMNS[kind] + g * 4 * HD + j * HD
                        sp.dma_start(w_raw[:, b, :, g * HD:(g + 1) * HD], w_cols[:, :, c:c + HD]).then_inc(w_in_s[b], 16)
                    else:
                        c = COLUMNS[kind] + j * P
                        k = slice(g * KD // 2, (g + 1) * KD // 2)
                        sp.dma_start(w_raw[:, b, k, :], w_cols[:, k, c:c + P]).then_inc(w_in_s[b], 16)

            sp.dma_start(x_in[:, 0, :], x_rows[:, 0, :]).then_inc(x_in_s[0], 16)
            sp.dma_start(norm_row, norm_w[0:1, :].broadcast_to([P, D])).then_inc(norm_in, 16)
            sp.dma_start(x_in[:, 1, :], x_rows[:, 1, :]).then_inc(x_in_s[1], 16)
            load_w(0)
            for b in range(2, 4):
                sp.dma_start(x_in[:, b, :], x_rows[:, b, :]).then_inc(x_in_s[b], 16)
            load_w(1)
            for dst, src in ((lam_in[:, 0], lq1[0:1, :].broadcast_to([P, HD])),
                             (lam_in[:, 1], lk1[0:1, :].broadcast_to([P, HD])),
                             (lam_in[:, 2], lq2[0:1, :].broadcast_to([P, HD])),
                             (lam_in[:, 3], lk2[0:1, :].broadcast_to([P, HD])),
                             (sub_w[:], subln_w.rearrange("l e -> e l")),
                             (sink[:], sinks[0:1, :].broadcast_to([P, 8]))):
                sp.dma_start(dst, src).then_inc(const_in, 16)
            sp.dma_start(cos[:], cos_t).then_inc(table_in, 16)
            sp.dma_start(sin[:], sin_t).then_inc(table_in, 16)
            for st in PLAN:
                if st[0] == "xturn" and st[1] + 4 < NS:
                    s = st[1] + 4
                    sp.wait_ge(turn_ok, 2 * st[1] + 2)
                    sp.dma_start(x_in[:, s % 4, :], x_rows[:, s, :]).then_inc(x_in_s[s % 4], 16)
                if st[0] == "split":
                    load_w(st[1] + 2)
                if st[0] == "copy" and TILES[st[1][0]][0] in ROTARY:
                    n = number[st[1]]
                    sp.wait_ge(copy_ok, n + 1)
                    for q in range(4):
                        to, fr = 32 * q, 32 * (q ^ 1)
                        sp.dma_start(swp[to:to + 32, n % 2, :], raw[fr:fr + 32, n % 2, :]).then_inc(swap_s[n % 2], 16)
                if st == ("msplit", 0):
                    sp.wait_ge(rope_ok, count(len(projs), ROTARY))
                    sp.dma_start(fin_w[:], final_w.rearrange("(o d) -> o d", o=1).broadcast_to([P, D])).then_inc(fin_in, 16)
                    sp.wait_ge(proj_ok, len(projs))
                    for b in range(2):
                        sp.dma_start(x_again[:, b, :], x_rows[:, b, :]).then_inc(x_again_s[b], 16)
                if st[0] == "result":
                    i = st[1]
                    sp.wait_ge(res_ok, i + 1)
                    sp.dma_start(out_rows[:, i, :], res[:, i % 2, :]).then_inc(stored[i % 2], 16)
                    if i + 2 < NS:
                        sp.dma_start(x_again[:, i % 2, :], x_rows[:, i + 2, :]).then_inc(x_again_s[i % 2], 16)
            for b in range(2):
                sp.wait_ge(stored[b], 16 * NS // 2)

        @block.tensor
        def _(pe):
            def turn(t, blocks):
                n = turn_no[t]
                if n >= 2 and turns[n - 2][0] in ("x", "o"):
                    pe.wait_ge(turn_dve, turns_read(n - 2, ("x", "o")))
                elif n >= 2:
                    pe.wait_ge(turn_act, turns_read(n - 2, ("a", "v")))
                for k, src in enumerate(blocks):
                    tr = pe.transpose(pT[:, n % 2, k * P:(k + 1) * P], src, ident[:])
                tr.then_inc(turn_ok, 1)

            pe.wait_ge(const_ok, 1)
            for st in PLAN:
                if st[0] == "xturn":
                    s = st[1]
                    pe.wait_ge(x_norm, s + 1)
                    for r in range(2):
                        turn(("x", s, r), [x_in[:, s % 4, (4 * r + k) * P:(4 * r + k + 1) * P] for k in range(4)])
                if st[0] == "proj":
                    (t, half), a, b = st[1:]
                    n = number[st[1]]
                    if a == 0:
                        if half == 0:
                            pe.wait_ge(w_hi_ok, t + 1)
                            pe.wait_ge(w_lo_ok, t + 1)
                        if t == 0:
                            pe.wait_ge(turn_dve, NS * (half + 1))
                        wait_bank_free(pe, n)
                    frames = slice(half * HALF, (half + 1) * HALF)
                    for q in range(a, b):
                        k, part = q // 3, q % 3
                        w = (w_hi, w_hi, w_lo)[part][:, t % 2, k, :]
                        xt = (xT_hi, xT_lo, xT_hi)[part][:, k, frames]
                        mm = pe.matmul(bank(n), w, xt, start=(q == 0), stop=(q == 3 * KD - 1))
                    if b == 3 * KD:
                        mm.then_inc(proj_ok, 1)
                if st[0] == "place" and TILES[st[1][0]][0] in VALUE:
                    n = number[st[1]]
                    pe.wait_ge(copy_ok, n + 1)
                    turn(("v", st[1]), [raw[:, n % 2, k * P:(k + 1) * P] for k in range(4)])
                if st[0] == "place" and TILES[st[1][0]][0] == "gb":
                    t, half = st[1]
                    h = TILES[t][1]
                    pe.wait_ge(o_norm, 2 * h + half + 1)
                    turn(("o", st[1]), [o_b[:, h, 4 * half + k, :] for k in range(4)])
                if st[0] == "scores" and st[1] < WA:
                    w, m = st[1:]
                    h, i = w // NS, w % NS
                    if i in (0, NS // 2):
                        pe.wait_ge(rope_ok, count(tile_done("qb", h, 2 * i // NS), ROTARY))
                    if w == 0:
                        pe.wait_ge(copy_ok, PROLOGUE)
                    else:
                        pe.wait_ge(exp_ok[m], w)
                    keys = (i + 1) * P
                    for c in range(0, keys, HALF):
                        e = min(keys, c + HALF)
                        mm = pe.matmul(pS[:, m, c:e], qb[:, h % 2, i * P:(i + 1) * P], kb[:, h % 2, m, c:e],
                                       start=True, stop=True)
                    mm.then_inc(scores_ok[m], 1)
                if st[0] == "scores" and st[1] >= WA:
                    w, m = st[1:]
                    i = (w - WA) // 2
                    if i == 0:
                        pe.wait_ge(rope_ok, count(tile_done("qa", 3), ROTARY))
                    pe.wait_ge(exp_ok[m], visit(w))
                    c, nk = columns_a(i)
                    for t in range(4):
                        mm = pe.matmul(pS_a[:, m, t, c:c + nk], qa[:, t, i * P:(i + 1) * P],
                                       ka[:, m, (i + 1) * P - nk:(i + 1) * P], start=True, stop=True)
                    mm.then_inc(scores_ok[m], 1)
                if st[0] == "turns":
                    w = st[1]
                    pe.wait_ge(at_ok, w + 1)
                    for t in turns_of(w):
                        if w < WA:
                            turn(t, [at[:, w % 2, k * P:(k + 1) * P]
                                     for k in range(4 * t[2], min(4 * t[2] + 4, w % NS + 1))])
                        else:
                            c = (t[2] if w >= WA + 2 else 1) * P
                            turn(t, [at_a[:, w % 2, hh, c:c + P] for hh in range(4)])
                if st[0] == "values":
                    w = st[1]
                    if o_visit(w) >= 1 and (w >= WA or w % 4 == 0):
                        pe.wait_ge(o_copied, o_visit(w))
                    for t in turns_of(w):
                        pe.wait_ge(turn_act, turns_read(turn_no[t], ("a", "v")))
                        src = aT[:, att_no[t] % 2, :]
                        if w < WA:
                            h, i = w // NS, w % NS
                            if i in (0, 4) and t[2] == 0:
                                v = ("v", (TILES.index(("vb", h)), i // 4))
                                pe.wait_ge(turn_act, turns_read(turn_no[v], ("a", "v")))
                            for k in range(4 * t[2], min(4 * t[2] + 4, i + 1)):
                                mm = pe.matmul(pO[:, (i % 4) * P:(i % 4 + 1) * P], src[:, (k % 4) * P:(k % 4 + 1) * P],
                                               vb[:, h % 2, k, :], start=(k == 0), stop=(k == i))
                        else:
                            i = (w - WA) // 2
                            if i == 0:
                                v = ("v", (TILES.index(("va", 0)), 1))
                                pe.wait_ge(turn_act, turns_read(turn_no[v], ("a", "v")))
                            k = i - len(turns_of(w)) + 1 + t[2]
                            mm = pe.matmul(pO[:, :], va[:, k, :], src, start=(t is turns_of(w)[0]),
                                           stop=(t is turns_of(w)[-1]))
                        mm.then_inc(av_ok, 1)
                if st[0] == "out":
                    i = st[1]
                    b = i % 2
                    if i == 0:
                        pe.wait_ge(copy_ok, len(projs))
                        pe.wait_ge(gate_ok, count(len(projs), GATE))
                        pe.wait_ge(w_hi_ok, NT + KD)
                        pe.wait_ge(w_lo_ok, NT + KD)
                    if i >= 2:
                        pe.wait_ge(y_ok, i - 1)
                    pe.wait_ge(mlo_ok, i + 1)
                    for c in range(2):
                        cols = slice(c * HALF, (c + 1) * HALF)
                        for q in range(3 * KD):
                            k, part = q // 3, q % 3
                            mm = pe.matmul(pS[:, b, cols], (mix_hi, mix_hi, mix_lo)[part][:, b, k, :],
                                           (wo_hi, wo_lo, wo_hi)[part][:, k, cols], start=(q == 0), stop=(q == 3 * KD - 1))
                    mm.then_inc(out_ok, 1)

        @block.scalar
        def _(act):
            def copy(out_, in_, scale=1.0):
                return nc.scalar.activation(out_, in_, ACT.Copy, scale=scale)

            act.wait_ge(lam_dot, 2)
            nc.scalar.activation(lam_s[:, 2:4], lam_s[:, 0:2], ACT.Exp).then_inc(lam_exp, 1)
            for st in PLAN:
                if st[0] == "xnorm":
                    s = st[1]
                    act.wait_ge(x_in_s[s % 4], 16 * (s // 4 + 1))
                    if s:
                        act.wait_ge(x_ss, s)
                    nc.scalar.activation(pr[:, 0, :], x_in[:, s % 4, :], ACT.Square,
                                         accum_out=ss[:, 0, s:s + 1]).then_inc(x_ss, 1)
                if st[0] == "xturn":
                    s = st[1]
                    for r in range(2):
                        n = turn_no[("x", s, r)]
                        act.wait_ge(turn_ok, n + 1)
                        copy(xT_hi[:, 4 * r:4 * r + 4, s * P:(s + 1) * P],
                             pT[:, n % 2, :].rearrange("p (k s) -> p k s", k=4)).then_inc(xhi_ok, 1)
                if st[0] == "split":
                    n = st[1]
                    act.wait_ge(w_in_s[n % 2], 32 * (n // 2 + 1))
                    if n < NT:
                        if n >= 2:
                            act.wait_ge(proj_ok, 2 * (n - 1))
                        copy(w_hi[:, n % 2], w_raw[:, n % 2]).then_inc(w_hi_ok, 1)
                    else:
                        if n == NT:
                            act.wait_ge(av_ok, len(att_turns))
                        copy(wo_hi[:, n - NT, :], w_raw[:, n % 2].rearrange("p k c -> p (k c)")).then_inc(w_hi_ok, 1)
                if st[0] == "copy":
                    n = number[st[1]]
                    act.wait_ge(proj_ok, n + 1)
                    wait_stage_free(act, n)
                    if kind_of[n] in GATE:
                        nc.scalar.activation(raw[:, n % 2, :], bank(n), ACT.Tanh, scale=0.5).then_inc(copy_ok, 1)
                    else:
                        copy(raw[:, n % 2, :], bank(n), SCALE if kind_of[n][0] == "q" else 1.0).then_inc(copy_ok, 1)
                if st[0] == "place" and TILES[st[1][0]][0] in VALUE:
                    n = turn_no[("v", st[1])]
                    (t, half), j = st[1], TILES[st[1][0]][1]
                    act.wait_ge(turn_ok, n + 1)
                    if TILES[t][0] == "vb":
                        if j >= 2:
                            act.wait_ge(av_ok, sum(x_[1] < NS * (j - 1) for x_ in att_turns))
                        dst = vb[:, j % 2, 4 * half:4 * half + 4, :]
                    else:
                        dst = va[:, 4 * half:4 * half + 4, :]
                    copy(dst, pT[:, n % 2, :].rearrange("p (k s) -> p k s", k=4)).then_inc(turn_act, 1)
                if st[0] == "softmax":
                    w = st[1]
                    if w < WA:
                        keys = (w % NS + 1) * P
                        if w >= 1:
                            act.wait_ge(at_ok, w)
                        for m in range(2):
                            act.wait_ge(max_ok[m], w + 1)
                            nc.scalar.activation(pr[:, m, 0:keys], pS[:, m, 0:keys], ACT.Exp, bias=nmax[:, m, 0:1],
                                                 accum_out=rsum[:, m, 0:1]).then_inc(exp_ok[m], 1)
                    else:
                        m, i = w % 2, (w - WA) // 2
                        c, nk = columns_a(i)
                        act.wait_ge(at_ok, w if w < WA + 1 else w - 1)
                        act.wait_ge(max_ok[m], visit(w) + 1)
                        for t in range(4):
                            e = nc.scalar.activation(pr_a[:, m, t, c:c + nk], pS_a[:, m, t, c:c + nk], ACT.Exp,
                                                     bias=nmax[:, m, t:t + 1], accum_out=rsum[:, m, t:t + 1])
                        e.then_inc(exp_ok[m], 1)
                        nc.scalar.activation(esink[:, 1, :], esink[:, 0, :], ACT.Exp).then_inc(esink_ok, 1)
                if st[0] == "turns":
                    for t in turns_of(st[1]):
                        n, a = turn_no[t], att_no[t]
                        act.wait_ge(turn_ok, n + 1)
                        if a >= 2:
                            act.wait_ge(av_ok, a - 1)
                        width = P * min(4, st[1] % NS + 1 - 4 * t[2]) if st[1] < WA else HALF
                        copy(aT[:, a % 2, 0:width], pT[:, n % 2, 0:width]).then_inc(turn_act, 1)
                if st[0] == "values":
                    w = st[1]
                    if w >= WA or w % 4 == 3:
                        act.wait_ge(av_ok, att_no[turns_of(w)[-1]] + 1)
                    if w < WA and w % 4 == 3:
                        h, i = w // NS, w % NS
                        if w >= 7:
                            act.wait_ge(o_ss, w // 4)
                        nc.scalar.activation(o_sq[:], pO[:].rearrange("p (k e) -> p k e", k=4), ACT.Square)
                        copy(o_b[:, h, i - 3:i + 1, :], pO[:].rearrange("p (k e) -> p k e", k=4)).then_inc(o_copied, 1)
                    if w >= WA:
                        i, r = (w - WA) // 2, slice((w % 2) * HD, (w % 2 + 1) * HD)
                        copy(mixA[r, :, i * P:(i + 1) * P], pO[r, :].rearrange("p (k e) -> p k e", k=4)).then_inc(o_copied, 1)
                if st[0] == "msplit":
                    i = st[1]
                    act.wait_ge(proj_ok, len(projs))
                    act.wait_ge(turn_dve, turns_read(len(turns) - 1, ("x", "o")))
                    act.wait_ge(mixa_ok, 2 * NB)
                    if i >= 2:
                        act.wait_ge(out_ok, i - 1)
                    copy(mix_hi[:, i % 2, 0:4, :], mixA[:, :, i * P:(i + 1) * P])
                    copy(mix_hi[:, i % 2, 4:8, :], mixB[:, :, i * P:(i + 1) * P]).then_inc(mhi_ok, 1)
                if st[0] == "result":
                    i = st[1]
                    act.wait_ge(y_ok, i + 1)
                    if i >= 2:
                        act.wait_ge(stored[i % 2], 16 * (i // 2))
                    nc.scalar.activation(res[:, i % 2, :], y[:, i % 2, :], ACT.Square,
                                         accum_out=ss[:, 1, i:i + 1]).then_inc(y_ss, 1)

        @block.vector
        def _(dve):
            chain = [0]

            def link(ins):
                chain[0] += 1
                ins.then_inc(dve_chain, 1)
                dve.wait_ge(dve_chain, chain[0])

            dve.wait_ge(const_in, 16 * 6)
            for j in range(2):
                nc.vector.tensor_tensor_reduce(out=lam_junk[:, j], in0=lam_in[:, 2 * j], in1=lam_in[:, 2 * j + 1], scale=1.0,
                                               scalar=0.0, op0=ALU.mult, op1=ALU.add,
                                               accum_out=lam_s[:, j:j + 1]).then_inc(lam_dot, 1)
            link(nc.vector.tensor_scalar(neg_sink[:], sink[:], -1.0, None, ALU.mult))
            link(nc.vector.tensor_scalar(sub_ws[:], sub_w[:], (1.0 - LAMBDA_INIT) * 0.5, None, ALU.mult))
            dve.wait_ge(lam_exp, 1)
            link(nc.vector.tensor_tensor(lam_s[:, 4:5], lam_s[:, 2:3], lam_s[:, 3:4], ALU.subtract))
            link(nc.vector.tensor_scalar(neg_lam[:], lam_s[:, 4:5], -1.0, -LAMBDA_INIT, ALU.mult, ALU.add))

            for st in PLAN:
                if st[0] == "xnorm":
                    s = st[1]
                    if s == 0:
                        dve.wait_ge(norm_in, 16)
                    dve.wait_ge(x_rstd, s + 1)
                    nc.vector.scalar_tensor_tensor(out=x_in[:, s % 4, :], in0=x_in[:, s % 4, :], scalar=rstd[:, 0, s:s + 1],
                                                   in1=norm_row, op0=ALU.mult, op1=ALU.mult).then_inc(x_norm, 1)
                if st[0] == "xturn":
                    s = st[1]
                    for r in range(2):
                        n = turn_no[("x", s, r)]
                        dve.wait_ge(xhi_ok, 2 * s + r + 1)
                        hi = xT_hi[:, 4 * r:4 * r + 4, s * P:(s + 1) * P]
                        nc.vector.tensor_tensor(xT_lo[:, 4 * r:4 * r + 4, s * P:(s + 1) * P],
                                                pT[:, n % 2, :].rearrange("p (k s) -> p k s", k=4),
                                                hi.bitcast(F32), ALU.subtract).then_inc(turn_dve, 1)
                if st[0] == "copy" and TILES[st[1][0]][0] in GATE:
                    n = number[st[1]]
                    dve.wait_ge(copy_ok, n + 1)
                    wait_stage_free(dve, n)
                    nc.vector.scalar_tensor_tensor(out=swp[:, n % 2, :], in0=raw[:, n % 2, :], scalar=1.0, in1=bank(n),
                                                   op0=ALU.add, op1=ALU.mult).then_inc(gate_ok, 1)
                if st[0] == "place":
                    (t, half), n = st[1], number[st[1]]
                    kind, j = TILES[t]
                    frames = slice(half * HALF, (half + 1) * HALF)
                    if kind in ROTARY:
                        dve.wait_ge(rope_mul, count(n + 1, ROTARY))
                        if kind in ("qb", "kb") and j >= 2:
                            for m in range(2):
                                dve.wait_ge(scores_ok[m], NS * (j - 1))
                        if n == 0:
                            dve.wait_ge(const_ok, 1)
                        if kind == "qb":
                            places = [(slice(0, P), qb[:, j % 2, frames])]
                        elif kind == "qa":
                            places = [(slice(0, P), qa[:, j, frames])]
                        else:
                            half_rows = [slice(m * HD, (m + 1) * HD) for m in range(2)]
                            k_dst = kb[:, j % 2] if kind == "kb" else ka[:]
                            places = [(r, k_dst[r, m, frames]) for m, r in enumerate(half_rows)]
                        for rows, dst in places:
                            sum_ = nc.vector.tensor_tensor(dst, raw[rows, n % 2, :], swp[rows, n % 2, :], ALU.add)
                        sum_.then_inc(rope_ok, 1)
                    if kind == "gb":
                        tn = turn_no[("o", st[1])]
                        dve.wait_ge(turn_ok, tn + 1)
                        dve.wait_ge(gate_ok, count(n + 1, GATE))
                        nc.vector.scalar_tensor_tensor(out=mixB[:, j, frames], in0=pT[:, tn % 2, :], scalar=sub_ws[:, 0:1],
                                                       in1=swp[:, n % 2, :], op0=ALU.mult,
                                                       op1=ALU.mult).then_inc(turn_dve, 1)
                    if kind == "ga":
                        dve.wait_ge(o_copied, NS + 2 * NS)
                        dve.wait_ge(gate_ok, count(n + 1, GATE))
                        nc.vector.scalar_tensor_tensor(out=mixA[:, j, frames], in0=mixA[:, j, frames], scalar=0.5,
                                                       in1=swp[:, n % 2, :], op0=ALU.mult, op1=ALU.mult).then_inc(mixa_ok, 1)
                if st[0] == "softmax" and st[1] < WA:
                    w = st[1]
                    keys = (w % NS + 1) * P
                    for m in range(2):
                        dve.wait_ge(scores_ok[m], w + 1)
                        link(nc.vector.memset(pS[0:CHUNK, m, keys - CHUNK:keys], NEG))
                        nc.vector.tensor_reduce(nmax[:, m, 0:1], pS[:, m, 0:keys], AX_X, ALU.max,
                                                negate=True).then_inc(max_ok[m], 1)
                    for m in range(2):
                        dve.wait_ge(exp_ok[m], w + 1)
                    link(nc.vector.reciprocal(rinv[:, :, 0:1], rsum[:, :, 0:1]))
                    link(nc.vector.tensor_scalar(rinv[:, 1, 1:2], rinv[:, 1, 0:1], neg_lam[:, 0:1], None, ALU.mult))
                    link(nc.vector.tensor_scalar(pr[:, 1, 0:keys], pr[:, 1, 0:keys], rinv[:, 1, 1:2], None, ALU.mult))
                    if w >= 2:
                        dve.wait_ge(turn_ok, turn_no[turns_of(w - 2)[-1]] + 1)
                    nc.vector.scalar_tensor_tensor(out=at[:, w % 2, 0:keys], in0=pr[:, 0, 0:keys], scalar=rinv[:, 0, 0:1],
                                                   in1=pr[:, 1, 0:keys], op0=ALU.mult, op1=ALU.add).then_inc(at_ok, 1)
                if st[0] == "softmax" and st[1] >= WA:
                    w = st[1]
                    m, i = w % 2, (w - WA) // 2
                    c, nk = columns_a(i)
                    dve.wait_ge(scores_ok[m], visit(w) + 1)
                    link(nc.vector.memset(pS_a[0:CHUNK, m, :, 3 * CHUNK:4 * CHUNK], NEG))
                    if i > 0:
                        link(nc.vector.memset(pS_a[CHUNK:P, m, :, CHUNK:2 * CHUNK], NEG))
                    link(nc.vector.tensor_reduce(nmax[:, m, :], pS_a[:, m, :, c:c + nk], AX_X, ALU.max, negate=True))
                    link(nc.vector.tensor_tensor(nmax[:, m, :], nmax[:, m, :], neg_sink[:, 4 * m:4 * m + 4], ALU.min))
                    nc.vector.tensor_tensor(esink[:, 0, :], nmax[:, m, :], neg_sink[:, 4 * m:4 * m + 4],
                                            ALU.subtract).then_inc(max_ok[m], 1)
                    dve.wait_ge(exp_ok[m], visit(w) + 1)
                    dve.wait_ge(esink_ok, w - WA + 1)
                    link(nc.vector.tensor_tensor(rsum[:, m, :], rsum[:, m, :], esink[:, 1, :], ALU.add))
                    link(nc.vector.reciprocal(rinv[:, m, :], rsum[:, m, :]))
                    dve.wait_ge(turn_ok, turn_no[turns_of(w - 2)[-1]] + 1)
                    if w < WA + 2:
                        nc.vector.memset(at_a[:, m, :, 0:CHUNK], 0.0)
                    nc.vector.tensor_tensor(at_a[:, m, :, c:c + nk], pr_a[:, m, :, c:c + nk],
                                            rinv[:, m, :].unsqueeze(2).broadcast_to([P, 4, nk]), ALU.mult).then_inc(at_ok, 1)
                if st[0] == "values" and st[1] < WA and st[1] % 4 == 3:
                    v = o_visit(st[1])
                    dve.wait_ge(o_copied, v + 1)
                    nc.vector.tensor_reduce(o_stat(ss, v), o_sq[:], AX_X, ALU.add).then_inc(o_ss, 1)
                if st[0] == "values" and st[1] % 4 == 0 and 4 <= st[1] <= WA:
                    v = o_visit(st[1]) - 1 if st[1] < WA else NS - 1
                    dve.wait_ge(o_rstd, v + 1)
                    rows = o_b[:, v // 2, 4 * (v % 2):4 * (v % 2) + 4, :]
                    nc.vector.tensor_tensor(rows, rows, o_stat(rstd, v).unsqueeze(2).broadcast_to([P, 4, P]),
                                            ALU.mult).then_inc(o_norm, 1)
                if st[0] == "msplit":
                    i = st[1]
                    dve.wait_ge(mhi_ok, i + 1)
                    for g, mix in enumerate((mixA, mixB)):
                        lo = nc.vector.tensor_tensor(mix_lo[:, i % 2, 4 * g:4 * g + 4, :], mix[:, :, i * P:(i + 1) * P],
                                                     mix_hi[:, i % 2, 4 * g:4 * g + 4, :].bitcast(F32), ALU.subtract)
                    lo.then_inc(mlo_ok, 1)
                if st[0] == "result":
                    i = st[1]
                    b = i % 2
                    if i == 0:
                        dve.wait_ge(fin_in, 16)
                    dve.wait_ge(out_ok, i + 1)
                    dve.wait_ge(x_again_s[b], 16 * (i // 2 + 1))
                    nc.vector.tensor_tensor(y[:, b, :], pS[:, b, :], x_again[:, b, :], ALU.add).then_inc(y_ok, 1)
                    dve.wait_ge(y_rstd, i + 1)
                    nc.vector.scalar_tensor_tensor(out=res[:, b, :], in0=y[:, b, :], scalar=rstd[:, 1, i:i + 1],
                                                   in1=fin_w[:], op0=ALU.mult, op1=ALU.mult).then_inc(res_ok, 1)

        @block.gpsimd
        def _(pool):
            chain = [0]

            def link(ins):
                chain[0] += 1
                ins.then_inc(pool_chain, 1)
                pool.wait_ge(pool_chain, chain[0])

            def inverse_root(stat, sums, scale, eps, done):
                mean, root = stat
                link(nc.gpsimd.tensor_scalar(mean, sums, scale, eps, ALU.mult, ALU.add))
                nc.gpsimd.tensor_tensor(root, mean, minus_half[:, 0:root.shape[1]], ALU.pow).then_inc(done, 1)

            link(nc.gpsimd.memset(minus_half[:], -0.5))
            link(nc.gpsimd.memset(ident[:], 0.0))
            link(nc.gpsimd.affine_select(out=ident[:], in_=ident[:], compare_op=ALU.not_equal, fill=1.0, base=0,
                                         pattern=[[-1, P]], channel_multiplier=1))
            link(nc.gpsimd.memset(ka[:], 0.0))
            nc.gpsimd.memset(kb[:], 0.0).then_inc(const_ok, 1)
            for st in PLAN:
                if st[0] == "xnorm":
                    s = st[1]
                    pool.wait_ge(x_ss, s + 1)
                    inverse_root((ms[:, 0, s:s + 1], rstd[:, 0, s:s + 1]), ss[:, 0, s:s + 1], 1.0 / D, NORM_EPS, x_rstd)
                if st[0] == "split":
                    n = st[1]
                    pool.wait_ge(w_hi_ok, n + 1)
                    if n < NT:
                        nc.gpsimd.tensor_tensor(w_lo[:, n % 2], w_raw[:, n % 2], w_hi[:, n % 2].bitcast(F32),
                                                ALU.subtract).then_inc(w_lo_ok, 1)
                    else:
                        nc.gpsimd.tensor_tensor(wo_lo[:, n - NT, :], w_raw[:, n % 2].rearrange("p k c -> p (k c)"),
                                                wo_hi[:, n - NT, :].bitcast(F32), ALU.subtract).then_inc(w_lo_ok, 1)
                if st[0] == "copy" and TILES[st[1][0]][0] in ROTARY:
                    n = number[st[1]]
                    half = st[1][1]
                    frames = slice(half * HALF, (half + 1) * HALF)
                    if n == 0:
                        pool.wait_ge(table_in, 32)
                    pool.wait_ge(swap_s[n % 2], swaps(n))
                    nc.gpsimd.tensor_tensor(raw[:, n % 2, :], raw[:, n % 2, :], cos[:, frames], ALU.mult)
                    nc.gpsimd.tensor_tensor(swp[:, n % 2, :], swp[:, n % 2, :], sin[:, frames],
                                            ALU.mult).then_inc(rope_mul, 1)
                if st[0] == "values" and st[1] < WA and st[1] % 4 == 3:
                    v = o_visit(st[1])
                    pool.wait_ge(o_ss, v + 1)
                    inverse_root((o_stat(ms, v), o_stat(rstd, v)), o_stat(ss, v), 1.0 / P, SUBLN_EPS, o_rstd)
                if st[0] == "result":
                    i = st[1]
                    pool.wait_ge(y_ss, i + 1)
                    inverse_root((ms[:, 1, i:i + 1], rstd[:, 1, i:i + 1]), ss[:, 1, i:i + 1], 1.0 / D, NORM_EPS, y_rstd)


def rotary_tables():
    inv_freq = (1.0 / (np.float32(10000.0) ** (np.arange(0, HD, 2, dtype=np.float32) / np.float32(HD)))).astype(np.float32)
    freqs = np.arange(S, dtype=np.float32)[None, :] * inv_freq[:, None]
    c, s = np.cos(freqs.astype(np.float64)), np.sin(freqs.astype(np.float64))
    return (np.concatenate([c, c] * 2).astype(np.float32), np.concatenate([-s, s] * 2).astype(np.float32))


_INS = ["x", "norm_w", "w_in", "sinks", "lambda_q1", "lambda_k1", "lambda_q2", "lambda_k2", "subln_w", "w_o",
        "final_norm_w"]


def kernel(**inputs):
    import concourse.bacc as bacc
    from concourse.bass_utils import run_bass_kernel_spmd

    nc = bacc.Bacc("TRN2", target_bir_lowering=False, num_devices=1)
    arrays, args = {}, []
    cos_t, sin_t = rotary_tables()
    for name, a in [(n, inputs[n]) for n in _INS] + [("cos", cos_t), ("sin", sin_t)]:
        arrays[f"in_{name}"] = np.ascontiguousarray(a)
        args.append(nc.dram_tensor(f"in_{name}", arrays[f"in_{name}"].shape, F32, kind="ExternalInput").ap())
    args.append(nc.dram_tensor("out", (1, S, D), F32, kind="ExternalOutput").ap())
    build(nc, *args)
    r = run_bass_kernel_spmd(nc, [arrays], core_ids=[0])
    return r.results[0]["out"]
```

```python
from contextlib import ExitStack

import numpy as np

import concourse.bass as bass
from concourse import mybir

F32 = mybir.dt.float32
F32R = mybir.dt.float32r
ALU = mybir.AluOpType
ACT = mybir.ActivationFunctionType
AX_X = mybir.AxisListType.X

P = 128
S = 1024
D = 1024
HD = 64
KD = D // P
NS = S // P
HALF = 512
NEG = -1e30
CHUNK = 64
NB = 4
SCALE = HD ** -0.5
LAMBDA_INIT = 0.8 - 0.6
NORM_EPS = 1e-6
SUBLN_EPS = 1e-5
QA, KA, VA, GA, QB, KB, VB, GB = 0, 512, 640, 768, 1280, 1792, 2304, 2816


def weight_tiles():
    tiles = [("kb", 0), ("qb", 0), ("vb", 0)]
    for h, beside in zip(range(1, NB), (("va", 0), ("gb", 0), ("gb", 1))):
        tiles += [("kb", h), ("vb", h), ("qb", h), beside]
    tiles += [("qa", t) for t in range(4)] + [("ka", 0), ("gb", 2), ("gb", 3)] + [("ga", t) for t in range(4)]
    return tiles


TILES = weight_tiles()
NT = len(TILES)
STACKED = ("qb", "kb")
PROLOGUE = 4
WA = NB * NS
COLUMNS = {"qa": QA, "ka": KA, "va": VA, "ga": GA, "qb": QB, "kb": KB, "vb": VB, "gb": GB}


def make_plan():
    plan, waiting, unstacked, loads = [], [], [], []

    def project(half, a=0, b=3 * KD):
        plan.append(("proj", half, a, b))

    def evacuate(half):
        for n in loads:
            plan.append(("load", n + 2))
        loads.clear()
        plan.append(("copy", half))
        if half[1] == 1 and half[0] + 2 < NT:
            plan.append(("split", half[0] + 2))
            loads.append(half[0] + 2)
        waiting.append(half)

    def place(keep=0):
        while len(waiting) > keep:
            half = waiting.pop(0)
            plan.append(("place", half))
            if TILES[half[0]][0] in STACKED:
                unstacked.append(half)

    def stack():
        plan.extend(("stack", half) for half in unstacked)
        unstacked.clear()

    def settle(keep=0):
        place(keep)
        stack()

    def attend(w, ahead):
        for v in ahead[:-1]:
            plan.extend(("scores", v, m) for m in range(2) if v < WA or m == v % 2)
            plan.append(("softmax", v))
        for v in ahead[-1:]:
            plan.extend(("scores", v, m) for m in range(2) if v < WA or m == v % 2)
            plan.extend([("softmax", v)] if v < WA else [("values", w), ("softmax", v)])
        if w is not None and (not ahead or ahead[-1] < WA):
            plan.append(("values", w))

    plan += [("xsquare", s) for s in range(3)] + [("xnorm", 0)]
    for s in range(NS):
        plan += [("xsquare", s + 3)] if s + 3 < NS else []
        plan += [("xnorm", s + 1)] if s + 1 < NS else []
        plan += [("xturn", s)]
        plan += [("split", s - 2)] if s in (2, 3) else [("load", s - 2)] if s in (4, 5) else []
        if s >= 3:
            half, a = [((0, 0), 0), ((0, 0), 12), ((1, 0), 0), ((1, 0), 12), ((0, 1), 0)][s - 3]
            project(half, a, 12 + a if s < NS - 1 else 24)
            if s != 3 and s != 5:
                evacuate(half)
                settle(1)
    plan += [("lambda",)]
    for half in ((1, 1), (2, 0), (2, 1)):
        project(half)
        evacuate(half)
        settle(1)
        if half == (2, 0):
            attend(None, [0])
    settle()
    fills = []
    for h in range(1, NB):
        n = 3 + 4 * (h - 1)
        fills += [[x] for x in ((n, 0), (n, 1), (n + 1, 0), (n + 1, 1), (n + 2, 0), (n + 3, 0), (n + 2, 1), (n + 3, 1))]
    n = 3 + 4 * (NB - 1)
    fills += [[(n + t, 0), (n + t, 1)] for t in range(4)]
    fills += [[(t, h)] for t in range(n + 4, NT) for h in range(2)]
    steps = WA + 2 * NS
    fills += [[] for _ in range(steps - len(fills))]
    windowed_gates = 0
    for w in range(steps):
        fill = fills[w]
        if fill:
            project(fill[0])
            evacuate(fill[0])
        plan += [("turns", w)]
        stack()
        attend(w, [v for v in ([w + 1] if w < WA - 1 else [w + 1, w + 2] if w == WA - 1 else [w + 2]) if v < steps])
        place()
        if len(fill) == 2:
            project(fill[1])
            evacuate(fill[1])
            stack()
            place()
        if not fill and w >= WA:
            done = sum(st[0] == "split" for st in plan)
            for n in range(done, min(done + 2, NT + KD)):
                plan += [("split", n), ("load", n + 2)]
            ready = (w - WA + 1) // 2
            plan += [("gate", i) for i in range(windowed_gates, min(windowed_gates + 2, ready))]
            windowed_gates = min(windowed_gates + 2, ready)
    plan += [("gate", i) for i in range(windowed_gates, NS)]
    done = sum(st[0] == "split" for st in plan)
    for n in range(done, NT + KD):
        plan += [("split", n), ("load", n + 2)]
    plan += [("msplit", 0), ("msplit", 1)]
    for i in range(NS):
        plan += [("out", i), ("result", i)]
        plan += [("msplit", i + 2)] if i + 2 < NS else []
    return plan


PLAN = make_plan()


def build(nc, x, norm_w, w_in, sinks, lq1, lk1, lq2, lk2, subln_w, w_o, final_w, cos_t, sin_t, out):
    x_rows = x.rearrange("b (i p) d -> p (b i) d", p=P)
    out_rows = out.rearrange("b (i p) d -> p (b i) d", p=P)
    w_cols = w_in.rearrange("l (k p) c -> p (l k) c", p=P)

    with ExitStack() as ctx:
        def keep(name, shape, dt=F32):
            return ctx.enter_context(nc.sbuf_tensor(name, shape, dt))

        ident = keep("ident", [P, P])
        w_raw = keep("w_raw", [P, 2, KD, P])
        w_hi = keep("w_hi", [P, 2, KD, P], F32R)
        w_lo = keep("w_lo", [P, 2, KD, P], F32R)
        o_b = keep("o_b", [P, NB, NS, P])
        raw = keep("raw", [P, 2, HALF])
        swp = keep("swp", [P, 2, HALF])
        o_sq = keep("o_sq", [P, 4, P])
        minus_half = keep("minus_half", [P, 8])
        ss = keep("ss", [P, 6, 8])
        ms = keep("ms", [P, 6, 8])
        rstd = keep("rstd", [P, 6, 8])
        lam_in = keep("lam_in", [P, 4, HD])
        lam_s = keep("lam_s", [P, 8])
        lam_junk = keep("lam_junk", [P, 2, HD])
        neg_lam = keep("neg_lam", [P, 1])
        sub_w = keep("sub_w", [P, 1])
        sub_ws = keep("sub_ws", [P, 1])
        sink = keep("sink", [P, 8])
        neg_sink = keep("neg_sink", [P, 8])
        nmax = keep("nmax", [P, 2, 4])
        rsum = keep("rsum", [P, 2, 4])
        rinv = keep("rinv", [P, 2, 4])
        esink = keep("esink", [P, 2, 4])
        with ExitStack() as early:
            def first(name, shape, dt=F32):
                return early.enter_context(nc.sbuf_tensor(name, shape, dt))

            kb = first("kb", [P, 2, 2, S], F32R)
            qb = first("qb", [P, 2, 2, S], F32R)
            vb = first("vb", [P, 2, NS, P])
            qa = first("qa", [P, 4, S])
            va = first("va", [P, NS, P])
            pr = first("pr", [P, 2, S])
            at = first("at", [P, 2, S])
            aT = first("aT", [P, 2, HALF])
            cos = first("cos", [P, S])
            sin = first("sin", [P, S])
            xT_hi = first("xT_hi", [P, KD, S], F32R)
            xT_lo = first("xT_lo", [P, KD, S], F32R)
        with ExitStack() as tail:
            def last_of(name, shape, dt=F32):
                return tail.enter_context(nc.sbuf_tensor(name, shape, dt))

            ka = last_of("ka", [P, 2, S])
            mixA = last_of("mixA", [P, 4, S])
            gA = last_of("gA", [P, 4, S])
            mix_hi = last_of("mix_hi", [P, 2, KD, P], F32R)
            mix_lo = last_of("mix_lo", [P, 2, KD, P], F32R)
            x_again = last_of("x_again", [P, 2, D])
            y = last_of("y", [P, 2, D])
            res = last_of("res", [P, 2, D])
            fin_w = last_of("fin_w", [P, D])
            unused = last_of("unused", [P, D])
            wo_hi = last_of("wo_hi", [P, KD, D], F32R)
            wo_lo = last_of("wo_lo", [P, KD, D], F32R)
        x_in = o_b[:].rearrange("p h i e -> p (h i e)").rearrange("p (b d) -> p b d", d=D)
        mixB = o_b[:].rearrange("p h i e -> p h (i e)")
        norm_row = at[:, 1, :]
        at_a = at[:].rearrange("p b (h k) -> p b h k", h=4)
        pr_a = pr[:].rearrange("p b (h k) -> p b h k", h=4)

        def psum(name, shape):
            return ctx.enter_context(nc.psum_tensor(name, shape, F32))

        pS = psum("pS", [P, 2, 1024])
        pT = psum("pT", [P, 2, HALF])
        pO = psum("pO", [P, HALF])
        pP = psum("pP", [P, HALF])
        pS_a = pS[:].rearrange("p b (h k) -> p b h k", h=4)

        def sem(name):
            return ctx.enter_context(nc.semaphore(name))

        const_in = sem("const_in")
        norm_in = sem("norm_in")
        table_in = sem("table_in")
        x_in_s = [sem(f"x_in{b}") for b in range(4)]
        const_ok = sem("const_ok")
        lam_dot = sem("lam_dot")
        lam_exp = sem("lam_exp")
        x_ss = sem("x_ss")
        x_rstd = sem("x_rstd")
        x_norm = sem("x_norm")
        turn_ok = sem("turn_ok")
        turn_act = sem("turn_act")
        turn_dve = sem("turn_dve")
        xhi_ok = sem("xhi_ok")
        w_in_s = [sem(f"w_in{b}") for b in range(2)]
        w_hi_ok = sem("w_hi_ok")
        w_lo_ok = sem("w_lo_ok")
        proj_ok = sem("proj_ok")
        copy_ok = sem("copy_ok")
        gate_ok = sem("gate_ok")
        swap_s = [sem(f"swap{b}") for b in range(2)]
        rope_mul = sem("rope_mul")
        rope_ok = sem("rope_ok")
        stack_hi = sem("stack_hi")
        stack_lo = sem("stack_lo")
        stack_s = [sem(f"stack{b}") for b in range(2)]
        ka_zero = sem("ka_zero")
        scores_ok = [sem(f"scores_ok{m}") for m in range(2)]
        max_ok = [sem(f"max_ok{m}") for m in range(2)]
        exp_ok = [sem(f"exp_ok{m}") for m in range(2)]
        esink_ok = sem("esink_ok")
        at_ok = sem("at_ok")
        av_ok = sem("av_ok")
        o_copied = sem("o_copied")
        o_ss = sem("o_ss")
        o_rstd = sem("o_rstd")
        o_norm = sem("o_norm")
        mixa_ok = sem("mixa_ok")
        mhi_ok = sem("mhi_ok")
        mlo_ok = sem("mlo_ok")
        out_ok = sem("out_ok")
        y_ok = sem("y_ok")
        y_ss = sem("y_ss")
        y_rstd = sem("y_rstd")
        res_ok = sem("res_ok")
        x_again_s = [sem(f"x_again{b}") for b in range(2)]
        fin_in = sem("fin_in")
        stored = [sem(f"stored{b}") for b in range(2)]
        dve_chain = sem("dve_chain")
        pool_chain = sem("pool_chain")

        projs = [st[1] for st in PLAN if st[0] == "copy"]
        kind_of = [TILES[t][0] for t, _ in projs]
        number = {ph: n for n, ph in enumerate(projs)}
        n_attention = max(n for n, ph in enumerate(projs) if PLAN.index(("copy", ph)) < PLAN.index(("values", WA + 2 * NS - 1)))

        def count(n, kinds):
            return sum(k in kinds for k in kind_of[:n])

        ROTARY, VALUE, GATE = ("qa", "ka", "qb", "kb"), ("va", "vb"), ("ga", "gb")

        def bank_no(n):
            return n % 4 if n < PROLOGUE or n > n_attention else 4

        def bank(n):
            b = bank_no(n)
            return pP[:, :] if b == 4 else pS[:, b // 2, (b % 2) * HALF:(b % 2 + 1) * HALF]

        turns = []
        for st in PLAN:
            if st[0] == "xturn":
                turns += [("x", st[1], r) for r in range(2)]
            if st[0] == "place" and TILES[st[1][0]][0] in VALUE:
                turns.append(("v", st[1]))
            if st[0] == "place" and TILES[st[1][0]][0] == "gb":
                turns.append(("o", st[1]))
            if st[0] == "turns":
                w = st[1]
                n_turns = (w % NS + 4) // 4 if w < WA else (1 if w < WA + 2 else 2)
                turns += [("a", w, r) for r in range(n_turns)]
        turn_no = {t: n for n, t in enumerate(turns)}
        att_turns = [t for t in turns if t[0] == "a"]
        att_no = {t: n for n, t in enumerate(att_turns)}

        def turns_of(w):
            return [t for t in att_turns if t[1] == w]

        def turns_read(n, kinds):
            return sum(t[0] in kinds for t in turns[:n + 1])

        def wait_bank_free(pe, n):
            earlier = [j for j in range(n) if bank_no(j) == bank_no(n)]
            if earlier:
                pe.wait_ge(copy_ok, earlier[-1] + 1)
                if kind_of[earlier[-1]] in GATE:
                    pe.wait_ge(gate_ok, count(earlier[-1] + 1, GATE))
            if n > n_attention:
                pe.wait_ge(exp_ok[bank_no(n) // 2], WA + NS)

        def wait_stage_free(eng, n):
            if n < 2:
                return
            if kind_of[n - 2] == "gb":
                eng.wait_ge(turn_dve, turns_read(turn_no[("o", projs[n - 2])], ("x", "o")))
            elif kind_of[n - 2] == "ga":
                eng.wait_ge(gate_ok, count(n - 1, GATE))
            elif kind_of[n - 2] in VALUE:
                eng.wait_ge(turn_ok, turn_no[("v", projs[n - 2])] + 1)
            elif kind_of[n - 2] in STACKED:
                eng.wait_ge(stack_s[n % 2], stacked(n - 2))
            else:
                eng.wait_ge(rope_ok, count(n - 1, ROTARY))

        def swaps(n):
            return 64 * sum(kind_of[j] in ROTARY for j in range(n % 2, n + 1, 2))

        def stacked(n):
            return 16 * sum({"kb": 4, "qb": 8}.get(kind_of[j], 0) for j in range(n % 2, n + 1, 2))

        def tile_done(kind, j, half=1):
            return number[(TILES.index((kind, j)), half)] + 1

        def o_visit(w):
            return w // 4 if w < WA else NS + w - WA

        def visit(w):
            return w if w < WA else WA + (w - WA) // 2

        def o_stat(stat, v):
            return stat[:, 2 + v // 2, 4 * (v % 2):4 * (v % 2) + 4]

        def columns_a(i):
            return (P, P) if i == 0 else (CHUNK, P + CHUNK)

        block = ctx.enter_context(nc.Block())

        @block.sync
        def _(sp):
            def load_w(n):
                if n >= NT + KD:
                    return
                if n >= 2:
                    sp.wait_ge(w_hi_ok, n - 1)
                    sp.wait_ge(w_lo_ok, n - 1)
                b = n % 2
                if n >= NT:
                    e = n - NT
                    dst = w_raw[:, b].rearrange("p k c -> p (k c)")
                    for g in range(2):
                        r = g * 4 * HD + e * HD if e < 4 else e * P + g * HD
                        sp.dma_start(dst[g * HD:(g + 1) * HD], w_o[0, r:r + HD, :]).then_inc(w_in_s[b], 16)
                    return
                kind, j = TILES[n]
                for g in range(2):
                    if kind in ("qa", "ga"):
                        c = COLUMNS[kind] + g * 4 * HD + j * HD
                        sp.dma_start(w_raw[:, b, :, g * HD:(g + 1) * HD], w_cols[:, :, c:c + HD]).then_inc(w_in_s[b], 16)
                    else:
                        c = COLUMNS[kind] + j * P
                        k = slice(g * KD // 2, (g + 1) * KD // 2)
                        sp.dma_start(w_raw[:, b, k, :], w_cols[:, k, c:c + P]).then_inc(w_in_s[b], 16)

            sp.dma_start(x_in[:, 0, :], x_rows[:, 0, :]).then_inc(x_in_s[0], 16)
            sp.dma_start(norm_row, norm_w[0:1, :].broadcast_to([P, D])).then_inc(norm_in, 16)
            for b in range(1, 4):
                sp.dma_start(x_in[:, b, :], x_rows[:, b, :]).then_inc(x_in_s[b], 16)
            load_w(0)
            load_w(1)
            for dst, src in ((lam_in[:, 0], lq1[0:1, :].broadcast_to([P, HD])),
                             (lam_in[:, 1], lk1[0:1, :].broadcast_to([P, HD])),
                             (lam_in[:, 2], lq2[0:1, :].broadcast_to([P, HD])),
                             (lam_in[:, 3], lk2[0:1, :].broadcast_to([P, HD])),
                             (sub_w[:], subln_w.rearrange("l e -> e l")),
                             (sink[:], sinks[0:1, :].broadcast_to([P, 8]))):
                sp.dma_start(dst, src).then_inc(const_in, 16)
            sp.dma_start(cos[:], cos_t).then_inc(table_in, 16)
            sp.dma_start(sin[:], sin_t).then_inc(table_in, 16)
            for st in PLAN:
                if st[0] == "xturn" and st[1] + 4 < NS:
                    s = st[1] + 4
                    sp.wait_ge(turn_ok, 2 * st[1] + 2)
                    sp.dma_start(x_in[:, s % 4, :], x_rows[:, s, :]).then_inc(x_in_s[s % 4], 16)
                if st[0] == "load":
                    load_w(st[1])
                if st[0] == "copy" and TILES[st[1][0]][0] in ROTARY:
                    n = number[st[1]]
                    sp.wait_ge(copy_ok, n + 1)
                    for q in range(4):
                        to, fr = 32 * q, 32 * (q ^ 1)
                        sp.dma_start(swp[to:to + 32, n % 2, :], raw[fr:fr + 32, n % 2, :]).then_inc(swap_s[n % 2], 16)
                if st[0] == "stack":
                    (t, half), n = st[1], number[st[1]]
                    kind, j = TILES[t]
                    frames = slice(half * HALF, (half + 1) * HALF)
                    low, high = slice(0, HD), slice(HD, P)
                    hi, lo = swp[:, n % 2, :], raw[:, n % 2, :]
                    sp.wait_ge(stack_lo, count(n + 1, STACKED))
                    if kind == "kb":
                        if j >= 2:
                            for m in range(2):
                                sp.wait_ge(scores_ok[m], NS * (j - 1))
                        k = kb[:, j % 2].bitcast(F32)
                        copies = [(k[low, 0, frames], hi[low]), (k[high, 0, frames], lo[low]),
                                  (k[low, 1, frames], lo[high]), (k[high, 1, frames], hi[high])]
                    else:
                        if j >= 1:
                            for m in range(2):
                                sp.wait_ge(scores_ok[m], NS * (j - 1) + 4 * (half + 1))
                        q = qb[:].bitcast(F32)
                        copies = [(q[low, 0, 0, frames], hi[low]), (q[low, 1, 0, frames], lo[low]),
                                  (q[high, 0, 0, frames], lo[low]), (q[high, 1, 0, frames], hi[low]),
                                  (q[low, 0, 1, frames], lo[high]), (q[low, 1, 1, frames], hi[high]),
                                  (q[high, 0, 1, frames], hi[high]), (q[high, 1, 1, frames], lo[high])]
                    for dst, src in copies:
                        sp.dma_start(dst, src).then_inc(stack_s[n % 2], 16)
                if st == ("msplit", 0):
                    sp.wait_ge(rope_ok, count(len(projs), ROTARY))
                    sp.dma_start(fin_w[:], final_w.rearrange("(o d) -> o d", o=1).broadcast_to([P, D])).then_inc(fin_in, 16)
                    sp.wait_ge(av_ok, len(att_turns))
                    for b in range(2):
                        sp.dma_start(x_again[:, b, :], x_rows[:, b, :]).then_inc(x_again_s[b], 16)
                if st[0] == "result":
                    i = st[1]
                    sp.wait_ge(res_ok, i + 1)
                    sp.dma_start(out_rows[:, i, :], res[:, i % 2, :]).then_inc(stored[i % 2], 16)
                    if i + 2 < NS:
                        sp.dma_start(x_again[:, i % 2, :], x_rows[:, i + 2, :]).then_inc(x_again_s[i % 2], 16)
            for b in range(2):
                sp.wait_ge(stored[b], 16 * NS // 2)

        @block.tensor
        def _(pe):
            def turn(t, blocks):
                n = turn_no[t]
                if n >= 2 and turns[n - 2][0] in ("x", "o"):
                    pe.wait_ge(turn_dve, turns_read(n - 2, ("x", "o")))
                elif n >= 2:
                    pe.wait_ge(turn_act, turns_read(n - 2, ("a", "v")))
                for k, src in enumerate(blocks):
                    tr = pe.transpose(pT[:, n % 2, k * P:(k + 1) * P], src, ident[:])
                tr.then_inc(turn_ok, 1)

            pe.wait_ge(const_ok, 1)
            for st in PLAN:
                if st[0] == "xturn":
                    s = st[1]
                    pe.wait_ge(x_norm, s + 1)
                    for r in range(2):
                        turn(("x", s, r), [x_in[:, s % 4, (4 * r + k) * P:(4 * r + k + 1) * P] for k in range(4)])
                if st[0] == "proj":
                    (t, half), a, b = st[1:]
                    n = number[st[1]]
                    if a == 0:
                        if half == 0:
                            pe.wait_ge(w_hi_ok, t + 1)
                            pe.wait_ge(w_lo_ok, t + 1)
                        if t == 0:
                            pe.wait_ge(turn_dve, NS * (half + 1))
                        wait_bank_free(pe, n)
                    frames = slice(half * HALF, (half + 1) * HALF)
                    for q in range(a, b):
                        k, part = q // 3, q % 3
                        w = (w_hi, w_hi, w_lo)[part][:, t % 2, k, :]
                        xt = (xT_hi, xT_lo, xT_hi)[part][:, k, frames]
                        mm = pe.matmul(bank(n), w, xt, start=(q == 0), stop=(q == 3 * KD - 1))
                    if b == 3 * KD:
                        mm.then_inc(proj_ok, 1)
                if st[0] == "place" and TILES[st[1][0]][0] in VALUE:
                    n = number[st[1]]
                    pe.wait_ge(copy_ok, n + 1)
                    turn(("v", st[1]), [raw[:, n % 2, k * P:(k + 1) * P] for k in range(4)])
                if st[0] == "place" and TILES[st[1][0]][0] == "gb":
                    t, half = st[1]
                    h = TILES[t][1]
                    pe.wait_ge(o_norm, 2 * h + half + 1)
                    turn(("o", st[1]), [o_b[:, h, 4 * half + k, :] for k in range(4)])
                if st[0] == "scores" and st[1] < WA:
                    w, m = st[1:]
                    h, i = w // NS, w % NS
                    if i in (0, NS // 2) and m == 0:
                        for kind in ("kb", "qb"):
                            n = tile_done(kind, h, 2 * i // NS) - 1
                            pe.wait_ge(stack_s[n % 2], stacked(n))
                    if w == 0:
                        pe.wait_ge(copy_ok, PROLOGUE)
                    else:
                        pe.wait_ge(exp_ok[m], w)
                    keys = (i + 1) * P
                    for c in range(0, keys, HALF):
                        e = min(keys, c + HALF)
                        for v in range(2):
                            mm = pe.matmul(pS[:, m, c:e], qb[:, v, m, i * P:(i + 1) * P], kb[:, h % 2, m, c:e],
                                           start=(v == 0), stop=(v == 1))
                    mm.then_inc(scores_ok[m], 1)
                if st[0] == "scores" and st[1] >= WA:
                    w, m = st[1:]
                    i = (w - WA) // 2
                    if i == 0:
                        pe.wait_ge(rope_ok, count(tile_done("ka", 0), ROTARY))
                    pe.wait_ge(exp_ok[m], visit(w))
                    c, nk = columns_a(i)
                    for t in range(4):
                        mm = pe.matmul(pS_a[:, m, t, c:c + nk], qa[:, t, i * P:(i + 1) * P],
                                       ka[:, m, (i + 1) * P - nk:(i + 1) * P], start=True, stop=True)
                    mm.then_inc(scores_ok[m], 1)
                if st[0] == "turns":
                    w = st[1]
                    pe.wait_ge(at_ok, w + 1)
                    for t in turns_of(w):
                        if w < WA:
                            turn(t, [at[:, w % 2, k * P:(k + 1) * P]
                                     for k in range(4 * t[2], min(4 * t[2] + 4, w % NS + 1))])
                        else:
                            c = (t[2] if w >= WA + 2 else 1) * P
                            turn(t, [at_a[:, w % 2, hh, c:c + P] for hh in range(4)])
                if st[0] == "values":
                    w = st[1]
                    if o_visit(w) >= 1 and (w >= WA or w % 4 == 0):
                        pe.wait_ge(o_copied, o_visit(w))
                    for t in turns_of(w):
                        pe.wait_ge(turn_act, turns_read(turn_no[t], ("a", "v")))
                        src = aT[:, att_no[t] % 2, :]
                        if w < WA:
                            h, i = w // NS, w % NS
                            if i in (0, 4) and t[2] == 0:
                                v = ("v", (TILES.index(("vb", h)), i // 4))
                                pe.wait_ge(turn_act, turns_read(turn_no[v], ("a", "v")))
                            for k in range(4 * t[2], min(4 * t[2] + 4, i + 1)):
                                mm = pe.matmul(pO[:, (i % 4) * P:(i % 4 + 1) * P], src[:, (k % 4) * P:(k % 4 + 1) * P],
                                               vb[:, h % 2, k, :], start=(k == 0), stop=(k == i))
                        else:
                            i = (w - WA) // 2
                            if i == 0:
                                v = ("v", (TILES.index(("va", 0)), 1))
                                pe.wait_ge(turn_act, turns_read(turn_no[v], ("a", "v")))
                            k = i - len(turns_of(w)) + 1 + t[2]
                            mm = pe.matmul(pO[:, :], va[:, k, :], src, start=(t is turns_of(w)[0]),
                                           stop=(t is turns_of(w)[-1]))
                        mm.then_inc(av_ok, 1)
                if st[0] == "out":
                    i = st[1]
                    b = i % 2
                    if i == 0:
                        for m in range(2):
                            pe.wait_ge(exp_ok[m], WA + NS)
                        pe.wait_ge(w_hi_ok, NT + KD)
                        pe.wait_ge(w_lo_ok, NT + KD)
                    if i >= 2:
                        pe.wait_ge(y_ok, i - 1)
                    pe.wait_ge(mlo_ok, i + 1)
                    for c in range(2):
                        cols = slice(c * HALF, (c + 1) * HALF)
                        for q in range(3 * KD):
                            k, part = q // 3, q % 3
                            mm = pe.matmul(pS[:, b, cols], (mix_hi, mix_hi, mix_lo)[part][:, b, k, :],
                                           (wo_hi, wo_lo, wo_hi)[part][:, k, cols], start=(q == 0), stop=(q == 3 * KD - 1))
                    mm.then_inc(out_ok, 1)

        @block.scalar
        def _(act):
            def copy(out_, in_, scale=1.0):
                return nc.scalar.activation(out_, in_, ACT.Copy, scale=scale)

            for st in PLAN:
                if st[0] == "lambda":
                    act.wait_ge(lam_dot, 2)
                    nc.scalar.activation(lam_s[:, 2:4], lam_s[:, 0:2], ACT.Exp).then_inc(lam_exp, 1)
                if st[0] == "xsquare":
                    s = st[1]
                    act.wait_ge(x_in_s[s % 4], 16 * (s // 4 + 1))
                    if s:
                        act.wait_ge(x_ss, s)
                    nc.scalar.activation(pr[:, 0, :], x_in[:, s % 4, :], ACT.Square,
                                         accum_out=ss[:, 0, s:s + 1]).then_inc(x_ss, 1)
                if st[0] == "xturn":
                    s = st[1]
                    for r in range(2):
                        n = turn_no[("x", s, r)]
                        act.wait_ge(turn_ok, n + 1)
                        copy(xT_hi[:, 4 * r:4 * r + 4, s * P:(s + 1) * P],
                             pT[:, n % 2, :].rearrange("p (k s) -> p k s", k=4)).then_inc(xhi_ok, 1)
                if st[0] == "split":
                    n = st[1]
                    act.wait_ge(w_in_s[n % 2], 32 * (n // 2 + 1))
                    if n < NT:
                        if n >= 2:
                            act.wait_ge(proj_ok, number[(n - 2, 1)] + 1)
                        copy(w_hi[:, n % 2], w_raw[:, n % 2]).then_inc(w_hi_ok, 1)
                    else:
                        if n == NT:
                            act.wait_ge(proj_ok, len(projs))
                        copy(wo_hi[:, n - NT, :], w_raw[:, n % 2].rearrange("p k c -> p (k c)")).then_inc(w_hi_ok, 1)
                if st[0] == "copy":
                    n = number[st[1]]
                    act.wait_ge(proj_ok, n + 1)
                    wait_stage_free(act, n)
                    if kind_of[n] in GATE:
                        nc.scalar.activation(raw[:, n % 2, :], bank(n), ACT.Tanh, scale=0.5).then_inc(copy_ok, 1)
                    else:
                        copy(raw[:, n % 2, :], bank(n), SCALE if kind_of[n][0] == "q" else 1.0).then_inc(copy_ok, 1)
                if st[0] == "stack":
                    n = number[st[1]]
                    act.wait_ge(rope_ok, count(n + 1, ROTARY))
                    copy(swp[:, n % 2, :].bitcast(F32R), raw[:, n % 2, :]).then_inc(stack_hi, 1)
                if st[0] == "place" and TILES[st[1][0]][0] in VALUE:
                    n = turn_no[("v", st[1])]
                    (t, half), j = st[1], TILES[st[1][0]][1]
                    act.wait_ge(turn_ok, n + 1)
                    if TILES[t][0] == "vb":
                        if j >= 2:
                            act.wait_ge(av_ok, sum(x_[1] < NS * (j - 1) for x_ in att_turns))
                        dst = vb[:, j % 2, 4 * half:4 * half + 4, :]
                    else:
                        dst = va[:, 4 * half:4 * half + 4, :]
                    copy(dst, pT[:, n % 2, :].rearrange("p (k s) -> p k s", k=4)).then_inc(turn_act, 1)
                if st[0] == "softmax":
                    w = st[1]
                    if w < WA:
                        keys = (w % NS + 1) * P
                        if w >= 1:
                            act.wait_ge(at_ok, w)
                        for m in range(2):
                            act.wait_ge(max_ok[m], w + 1)
                            nc.scalar.activation(pr[:, m, 0:keys], pS[:, m, 0:keys], ACT.Exp, bias=nmax[:, m, 0:1],
                                                 accum_out=rsum[:, m, 0:1]).then_inc(exp_ok[m], 1)
                    else:
                        m, i = w % 2, (w - WA) // 2
                        c, nk = columns_a(i)
                        act.wait_ge(at_ok, w if w < WA + 1 else w - 1)
                        act.wait_ge(max_ok[m], visit(w) + 1)
                        for t in range(4):
                            e = nc.scalar.activation(pr_a[:, m, t, c:c + nk], pS_a[:, m, t, c:c + nk], ACT.Exp,
                                                     bias=nmax[:, m, t:t + 1], accum_out=rsum[:, m, t:t + 1])
                        e.then_inc(exp_ok[m], 1)
                        nc.scalar.activation(esink[:, 1, :], esink[:, 0, :], ACT.Exp).then_inc(esink_ok, 1)
                if st[0] == "turns":
                    for t in turns_of(st[1]):
                        n, a = turn_no[t], att_no[t]
                        act.wait_ge(turn_ok, n + 1)
                        if a >= 2:
                            act.wait_ge(av_ok, a - 1)
                        width = P * min(4, st[1] % NS + 1 - 4 * t[2]) if st[1] < WA else HALF
                        copy(aT[:, a % 2, 0:width], pT[:, n % 2, 0:width]).then_inc(turn_act, 1)
                if st[0] == "values":
                    w = st[1]
                    if w >= WA or w % 4 == 3:
                        act.wait_ge(av_ok, att_no[turns_of(w)[-1]] + 1)
                    if w < WA and w % 4 == 3:
                        h, i = w // NS, w % NS
                        if w >= 7:
                            act.wait_ge(o_ss, w // 4)
                        nc.scalar.activation(o_sq[:], pO[:].rearrange("p (k e) -> p k e", k=4), ACT.Square)
                        copy(o_b[:, h, i - 3:i + 1, :], pO[:].rearrange("p (k e) -> p k e", k=4)).then_inc(o_copied, 1)
                    if w >= WA:
                        i, r = (w - WA) // 2, slice((w % 2) * HD, (w % 2 + 1) * HD)
                        copy(mixA[r, :, i * P:(i + 1) * P], pO[r, :].rearrange("p (k e) -> p k e", k=4)).then_inc(o_copied, 1)
                if st[0] == "msplit":
                    i = st[1]
                    if i == 0:
                        act.wait_ge(av_ok, len(att_turns))
                        act.wait_ge(turn_dve, turns_read(len(turns) - 1, ("x", "o")))
                    act.wait_ge(mixa_ok, i + 1)
                    if i >= 2:
                        act.wait_ge(out_ok, i - 1)
                    copy(mix_hi[:, i % 2, 0:4, :], mixA[:, :, i * P:(i + 1) * P])
                    copy(mix_hi[:, i % 2, 4:8, :], mixB[:, :, i * P:(i + 1) * P]).then_inc(mhi_ok, 1)
                if st[0] == "result":
                    i = st[1]
                    act.wait_ge(y_ok, i + 1)
                    if i >= 2:
                        act.wait_ge(stored[i % 2], 16 * (i // 2))
                    nc.scalar.activation(res[:, i % 2, :], y[:, i % 2, :], ACT.Square,
                                         accum_out=ss[:, 1, i:i + 1]).then_inc(y_ss, 1)

        @block.vector
        def _(dve):
            chain = [0]

            def link(ins):
                chain[0] += 1
                ins.then_inc(dve_chain, 1)
                dve.wait_ge(dve_chain, chain[0])

            for st in PLAN:
                if st[0] == "lambda":
                    dve.wait_ge(const_in, 16 * 6)
                    for j in range(2):
                        nc.vector.tensor_tensor_reduce(out=lam_junk[:, j], in0=lam_in[:, 2 * j], in1=lam_in[:, 2 * j + 1], scale=1.0,
                                                       scalar=0.0, op0=ALU.mult, op1=ALU.add,
                                                       accum_out=lam_s[:, j:j + 1]).then_inc(lam_dot, 1)
                    link(nc.vector.tensor_scalar(neg_sink[:], sink[:], -1.0, None, ALU.mult))
                    link(nc.vector.tensor_scalar(sub_ws[:], sub_w[:], (1.0 - LAMBDA_INIT) * 0.5, None, ALU.mult))
                    dve.wait_ge(lam_exp, 1)
                    link(nc.vector.tensor_tensor(lam_s[:, 4:5], lam_s[:, 2:3], lam_s[:, 3:4], ALU.subtract))
                    link(nc.vector.tensor_scalar(neg_lam[:], lam_s[:, 4:5], -1.0, -LAMBDA_INIT, ALU.mult, ALU.add))
                if st[0] == "xnorm":
                    s = st[1]
                    if s == 0:
                        dve.wait_ge(norm_in, 16)
                    dve.wait_ge(x_rstd, s + 1)
                    nc.vector.scalar_tensor_tensor(out=x_in[:, s % 4, :], in0=x_in[:, s % 4, :], scalar=rstd[:, 0, s:s + 1],
                                                   in1=norm_row, op0=ALU.mult, op1=ALU.mult).then_inc(x_norm, 1)
                if st[0] == "xturn":
                    s = st[1]
                    for r in range(2):
                        n = turn_no[("x", s, r)]
                        dve.wait_ge(xhi_ok, 2 * s + r + 1)
                        hi = xT_hi[:, 4 * r:4 * r + 4, s * P:(s + 1) * P]
                        nc.vector.tensor_tensor(xT_lo[:, 4 * r:4 * r + 4, s * P:(s + 1) * P],
                                                pT[:, n % 2, :].rearrange("p (k s) -> p k s", k=4),
                                                hi.bitcast(F32), ALU.subtract).then_inc(turn_dve, 1)
                if st[0] == "split" and st[1] < NT:
                    n = st[1]
                    dve.wait_ge(w_hi_ok, n + 1)
                    nc.vector.tensor_tensor(w_lo[:, n % 2], w_raw[:, n % 2], w_hi[:, n % 2].bitcast(F32),
                                            ALU.subtract).then_inc(w_lo_ok, 1)
                if st[0] == "copy" and TILES[st[1][0]][0] in GATE:
                    n = number[st[1]]
                    dve.wait_ge(copy_ok, n + 1)
                    (t, half), j = st[1], TILES[st[1][0]][1]
                    if TILES[t][0] == "ga":
                        dve.wait_ge(av_ok, sum(x_[1] < WA for x_ in att_turns))
                        dst = gA[:, j, half * HALF:(half + 1) * HALF]
                    else:
                        dst = swp[:, n % 2, :]
                    nc.vector.scalar_tensor_tensor(out=dst, in0=raw[:, n % 2, :], scalar=1.0, in1=bank(n),
                                                   op0=ALU.add, op1=ALU.mult).then_inc(gate_ok, 1)
                if st[0] == "place":
                    (t, half), n = st[1], number[st[1]]
                    kind, j = TILES[t]
                    frames = slice(half * HALF, (half + 1) * HALF)
                    if kind in ROTARY:
                        if n == 0:
                            dve.wait_ge(table_in, 32)
                        dve.wait_ge(swap_s[n % 2], swaps(n))
                        link(nc.vector.tensor_tensor(raw[:, n % 2, :], raw[:, n % 2, :], cos[:, frames], ALU.mult))
                        dve.wait_ge(rope_mul, count(n + 1, ROTARY))
                        if kind in STACKED:
                            places = [(slice(0, P), raw[:, n % 2, :])]
                        elif kind == "qa":
                            places = [(slice(0, P), qa[:, j, frames])]
                        else:
                            half_rows = [slice(m * HD, (m + 1) * HD) for m in range(2)]
                            places = [(r, ka[r, m, frames]) for m, r in enumerate(half_rows)]
                            dve.wait_ge(ka_zero, 1)
                        for rows, dst in places:
                            sum_ = nc.vector.tensor_tensor(dst, raw[rows, n % 2, :], swp[rows, n % 2, :], ALU.add)
                        sum_.then_inc(rope_ok, 1)
                    if kind == "gb":
                        tn = turn_no[("o", st[1])]
                        dve.wait_ge(turn_ok, tn + 1)
                        dve.wait_ge(gate_ok, count(n + 1, GATE))
                        nc.vector.scalar_tensor_tensor(out=mixB[:, j, frames], in0=pT[:, tn % 2, :], scalar=sub_ws[:, 0:1],
                                                       in1=swp[:, n % 2, :], op0=ALU.mult,
                                                       op1=ALU.mult).then_inc(turn_dve, 1)
                if st[0] == "stack":
                    n = number[st[1]]
                    dve.wait_ge(stack_hi, count(n + 1, STACKED))
                    nc.vector.tensor_tensor(raw[:, n % 2, :].bitcast(F32R), raw[:, n % 2, :], swp[:, n % 2, :],
                                            ALU.subtract).then_inc(stack_lo, 1)
                if st[0] == "gate":
                    i = st[1]
                    dve.wait_ge(o_copied, NS + 2 * i + 2)
                    dve.wait_ge(gate_ok, count(len(projs), GATE))
                    rows = mixA[:, :, i * P:(i + 1) * P]
                    nc.vector.scalar_tensor_tensor(out=rows, in0=rows, scalar=0.5, in1=gA[:, :, i * P:(i + 1) * P],
                                                   op0=ALU.mult, op1=ALU.mult).then_inc(mixa_ok, 1)
                if st[0] == "softmax" and st[1] < WA:
                    w = st[1]
                    keys = (w % NS + 1) * P
                    for m in range(2):
                        dve.wait_ge(scores_ok[m], w + 1)
                        link(nc.vector.memset(pS[0:CHUNK, m, keys - CHUNK:keys], NEG))
                        nc.vector.tensor_reduce(nmax[:, m, 0:1], pS[:, m, 0:keys], AX_X, ALU.max,
                                                negate=True).then_inc(max_ok[m], 1)
                    for m in range(2):
                        dve.wait_ge(exp_ok[m], w + 1)
                    link(nc.vector.reciprocal(rinv[:, :, 0:1], rsum[:, :, 0:1]))
                    link(nc.vector.tensor_scalar(rinv[:, 1, 1:2], rinv[:, 1, 0:1], neg_lam[:, 0:1], None, ALU.mult))
                    link(nc.vector.tensor_scalar(pr[:, 1, 0:keys], pr[:, 1, 0:keys], rinv[:, 1, 1:2], None, ALU.mult))
                    if w >= 2:
                        dve.wait_ge(turn_ok, turn_no[turns_of(w - 2)[-1]] + 1)
                    nc.vector.scalar_tensor_tensor(out=at[:, w % 2, 0:keys], in0=pr[:, 0, 0:keys], scalar=rinv[:, 0, 0:1],
                                                   in1=pr[:, 1, 0:keys], op0=ALU.mult, op1=ALU.add).then_inc(at_ok, 1)
                if st[0] == "softmax" and st[1] >= WA:
                    w = st[1]
                    m, i = w % 2, (w - WA) // 2
                    c, nk = columns_a(i)
                    dve.wait_ge(scores_ok[m], visit(w) + 1)
                    link(nc.vector.memset(pS_a[0:CHUNK, m, :, 3 * CHUNK:4 * CHUNK], NEG))
                    if i > 0:
                        link(nc.vector.memset(pS_a[CHUNK:P, m, :, CHUNK:2 * CHUNK], NEG))
                    link(nc.vector.tensor_reduce(nmax[:, m, :], pS_a[:, m, :, c:c + nk], AX_X, ALU.max, negate=True))
                    link(nc.vector.tensor_tensor(nmax[:, m, :], nmax[:, m, :], neg_sink[:, 4 * m:4 * m + 4], ALU.min))
                    nc.vector.tensor_tensor(esink[:, 0, :], nmax[:, m, :], neg_sink[:, 4 * m:4 * m + 4],
                                            ALU.subtract).then_inc(max_ok[m], 1)
                    dve.wait_ge(exp_ok[m], visit(w) + 1)
                    dve.wait_ge(esink_ok, w - WA + 1)
                    link(nc.vector.tensor_tensor(rsum[:, m, :], rsum[:, m, :], esink[:, 1, :], ALU.add))
                    link(nc.vector.reciprocal(rinv[:, m, :], rsum[:, m, :]))
                    dve.wait_ge(turn_ok, turn_no[turns_of(w - 2)[-1]] + 1)
                    if w < WA + 2:
                        nc.vector.memset(at_a[:, m, :, 0:CHUNK], 0.0)
                    nc.vector.tensor_tensor(at_a[:, m, :, c:c + nk], pr_a[:, m, :, c:c + nk],
                                            rinv[:, m, :].unsqueeze(2).broadcast_to([P, 4, nk]), ALU.mult).then_inc(at_ok, 1)
                if st[0] == "values" and st[1] < WA and st[1] % 4 == 3:
                    v = o_visit(st[1])
                    dve.wait_ge(o_copied, v + 1)
                    nc.vector.tensor_reduce(o_stat(ss, v), o_sq[:], AX_X, ALU.add).then_inc(o_ss, 1)
                if st[0] == "values" and st[1] % 4 == 0 and 4 <= st[1] <= WA:
                    v = o_visit(st[1]) - 1 if st[1] < WA else NS - 1
                    dve.wait_ge(o_rstd, v + 1)
                    rows = o_b[:, v // 2, 4 * (v % 2):4 * (v % 2) + 4, :]
                    nc.vector.tensor_tensor(rows, rows, o_stat(rstd, v).unsqueeze(2).broadcast_to([P, 4, P]),
                                            ALU.mult).then_inc(o_norm, 1)
                if st[0] == "msplit":
                    i = st[1]
                    dve.wait_ge(mhi_ok, i + 1)
                    for g, mix in enumerate((mixA, mixB)):
                        lo = nc.vector.tensor_tensor(mix_lo[:, i % 2, 4 * g:4 * g + 4, :], mix[:, :, i * P:(i + 1) * P],
                                                     mix_hi[:, i % 2, 4 * g:4 * g + 4, :].bitcast(F32), ALU.subtract)
                    lo.then_inc(mlo_ok, 1)
                if st[0] == "result":
                    i = st[1]
                    b = i % 2
                    if i == 0:
                        dve.wait_ge(fin_in, 16)
                    dve.wait_ge(out_ok, i + 1)
                    dve.wait_ge(x_again_s[b], 16 * (i // 2 + 1))
                    nc.vector.tensor_tensor(y[:, b, :], pS[:, b, :], x_again[:, b, :], ALU.add).then_inc(y_ok, 1)
                    dve.wait_ge(y_rstd, i + 1)
                    nc.vector.scalar_tensor_tensor(out=res[:, b, :], in0=y[:, b, :], scalar=rstd[:, 1, i:i + 1],
                                                   in1=fin_w[:], op0=ALU.mult, op1=ALU.mult).then_inc(res_ok, 1)

        @block.gpsimd
        def _(pool):
            chain = [0]

            def link(ins):
                chain[0] += 1
                ins.then_inc(pool_chain, 1)
                pool.wait_ge(pool_chain, chain[0])

            def inverse_root(stat, sums, scale, eps, done):
                mean, root = stat
                link(nc.gpsimd.tensor_scalar(mean, sums, scale, eps, ALU.mult, ALU.add))
                nc.gpsimd.tensor_tensor(root, mean, minus_half[:, 0:root.shape[1]], ALU.pow).then_inc(done, 1)

            link(nc.gpsimd.memset(minus_half[:], -0.5))
            link(nc.gpsimd.memset(ident[:], 0.0))
            nc.gpsimd.affine_select(out=ident[:], in_=ident[:], compare_op=ALU.not_equal, fill=1.0, base=0,
                                    pattern=[[-1, P]], channel_multiplier=1).then_inc(const_ok, 1)
            for st in PLAN:
                if st[0] == "xnorm":
                    s = st[1]
                    pool.wait_ge(x_ss, s + 1)
                    inverse_root((ms[:, 0, s:s + 1], rstd[:, 0, s:s + 1]), ss[:, 0, s:s + 1], 1.0 / D, NORM_EPS, x_rstd)
                if st[0] == "split" and st[1] >= NT:
                    n = st[1]
                    pool.wait_ge(w_hi_ok, n + 1)
                    nc.gpsimd.tensor_tensor(wo_lo[:, n - NT, :], w_raw[:, n % 2].rearrange("p k c -> p (k c)"),
                                            wo_hi[:, n - NT, :].bitcast(F32), ALU.subtract).then_inc(w_lo_ok, 1)
                if st[0] == "copy" and TILES[st[1][0]][0] in ROTARY:
                    n = number[st[1]]
                    half = st[1][1]
                    frames = slice(half * HALF, (half + 1) * HALF)
                    if n == 0:
                        pool.wait_ge(table_in, 32)
                    pool.wait_ge(swap_s[n % 2], swaps(n))
                    nc.gpsimd.tensor_tensor(swp[:, n % 2, :], swp[:, n % 2, :], sin[:, frames],
                                            ALU.mult).then_inc(rope_mul, 1)
                if st == ("values", 3 * NS - 1):
                    for m in range(2):
                        pool.wait_ge(scores_ok[m], 3 * NS)
                    nc.gpsimd.memset(ka[:], 0.0).then_inc(ka_zero, 1)
                if st[0] == "values" and st[1] < WA and st[1] % 4 == 3:
                    v = o_visit(st[1])
                    pool.wait_ge(o_ss, v + 1)
                    inverse_root((o_stat(ms, v), o_stat(rstd, v)), o_stat(ss, v), 1.0 / P, SUBLN_EPS, o_rstd)
                if st[0] == "result":
                    i = st[1]
                    pool.wait_ge(y_ss, i + 1)
                    inverse_root((ms[:, 1, i:i + 1], rstd[:, 1, i:i + 1]), ss[:, 1, i:i + 1], 1.0 / D, NORM_EPS, y_rstd)


def rotary_tables():
    inv_freq = (1.0 / (np.float32(10000.0) ** (np.arange(0, HD, 2, dtype=np.float32) / np.float32(HD)))).astype(np.float32)
    freqs = np.arange(S, dtype=np.float32)[None, :] * inv_freq[:, None]
    c, s = np.cos(freqs.astype(np.float64)), np.sin(freqs.astype(np.float64))
    return (np.concatenate([c, c] * 2).astype(np.float32), np.concatenate([-s, s] * 2).astype(np.float32))


_INS = ["x", "norm_w", "w_in", "sinks", "lambda_q1", "lambda_k1", "lambda_q2", "lambda_k2", "subln_w", "w_o",
        "final_norm_w"]


def kernel(**inputs):
    import concourse.bacc as bacc
    from concourse.bass_utils import run_bass_kernel_spmd

    nc = bacc.Bacc("TRN2", target_bir_lowering=False, num_devices=1)
    arrays, args = {}, []
    cos_t, sin_t = rotary_tables()
    for name, a in [(n, inputs[n]) for n in _INS] + [("cos", cos_t), ("sin", sin_t)]:
        arrays[f"in_{name}"] = np.ascontiguousarray(a)
        args.append(nc.dram_tensor(f"in_{name}", arrays[f"in_{name}"].shape, F32, kind="ExternalInput").ap())
    args.append(nc.dram_tensor("out", (1, S, D), F32, kind="ExternalOutput").ap())
    build(nc, *args)
    r = run_bass_kernel_spmd(nc, [arrays], core_ids=[0])
    return r.results[0]["out"]
```

```python
from contextlib import ExitStack

import numpy as np

from concourse import mybir

F32 = mybir.dt.float32
F32R = mybir.dt.float32r
ALU = mybir.AluOpType
ACT = mybir.ActivationFunctionType
AX_X = mybir.AxisListType.X

P = 128
S = 1024
D = 1024
HD = 64
KD = D // P
NS = S // P
HALF = 512
NEG = -1e30
CHUNK = 64
NB = 4
SCALE = HD ** -0.5
LAMBDA_INIT = 0.8 - 0.6
NORM_EPS = 1e-6
SUBLN_EPS = 1e-5
QA, KA, VA, GA, QB, KB, VB, GB = 0, 512, 640, 768, 1280, 1792, 2304, 2816


def weight_tiles():
    tiles = [("kb", 0), ("qb", 0), ("vb", 0)]
    for h, beside in zip(range(1, NB), (("va", 0), ("qa", 0), ("qa", 1))):
        tiles += [("kb", h), ("vb", h), ("qb", h), beside]
    tiles += [("qa", 2), ("qa", 3), ("ka", 0), ("gb", 0)] + [("ga", t) for t in range(4)]
    tiles += [("gb", h) for h in range(1, NB)]
    return tiles


TILES = weight_tiles()
NT = len(TILES)
STACKED = ("qb", "kb")
DVE_SPLITS = (2, 3)
PROLOGUE = 4
WA = NB * NS
COLUMNS = {"qa": QA, "ka": KA, "va": VA, "ga": GA, "qb": QB, "kb": KB, "vb": VB, "gb": GB}


def make_plan():
    plan, waiting, unstacked, loads = [], [], [], []

    def project(half, a=0, b=3 * KD):
        plan.append(("proj", half, a, b))

    def evacuate(half):
        for n in loads:
            plan.append(("load", n + 2))
        loads.clear()
        plan.append(("copy", half))
        waiting.append(half)

    def refill(half):
        if half[1] == 1 and half[0] + 2 < NT:
            plan.append(("split", half[0] + 2))
            loads.append(half[0] + 2)

    def place(keep=0):
        while len(waiting) > keep:
            half = waiting.pop(0)
            plan.append(("place", half))
            if TILES[half[0]][0] in STACKED:
                unstacked.append(half)

    def stack():
        plan.extend(("stack", half) for half in unstacked)
        unstacked.clear()

    def settle(keep=0):
        place(keep)
        stack()

    def attend(ahead):
        for v in ahead:
            plan.extend(("scores", v, m) for m in range(2) if v < WA or m == v % 2)
            plan.append(("softmax", v))

    plan += [(st, s) for s in range(3) for st in ("xsquare", "xroot")] + [("xnorm", 0)]
    for s in range(NS):
        plan += [("xsquare", s + 3), ("xroot", s + 3)] if s + 3 < NS else []
        plan += [("xnorm", s + 1)] if s + 1 < NS else []
        plan += [("xturn", s)]
        plan += [("split", s - 1)] if s in (1, 2) else [("load", s - 2)] if s in (4, 5) else []
        if s == NS - 1:
            plan += [("lambda",)]
        if s >= 3:
            half, a, b = [((0, 0), 0, 8), ((0, 0), 8, 16), ((0, 0), 16, 24), ((1, 0), 0, 12), ((1, 0), 12, 24)][s - 3]
            project(half, a, b)
            if b == 24:
                evacuate(half)
                settle(1)
    for half in ((0, 1), (1, 1), (2, 0), (2, 1)):
        project(half)
        evacuate(half)
        settle(1)
        if half == (2, 0):
            attend([0])
        refill(half)
    settle()
    fills = []
    for h in range(1, NB):
        n = 3 + 4 * (h - 1)
        fills += [(n, 0), (n, 1), (n + 1, 0), (n + 1, 1), (n + 2, 0), (n + 3, 0), (n + 2, 1), (n + 3, 1)]
    fills += [(t, h) for t in range(3 + 4 * (NB - 1), NT) for h in range(2)]
    steps = WA + 2 * NS
    windowed_gates = 0
    for w in range(steps - 2):
        half = fills[w]
        project(half, 0, 8)
        if w >= 1:
            plan += [("values", w - 1)]
        project(half, 8)
        evacuate(half)
        plan += [("turns", w)]
        stack()
        if w == len(fills) - 1:
            place()
            plan += [("scores", w + 2, (w + 2) % 2), ("values", w), ("turns", w + 1), ("softmax", w + 2)]
        else:
            attend([w + 1] if w < WA - 1 else [w + 1, w + 2] if w == WA - 1 else [w + 2])
        refill(half)
        place()
        if w >= len(fills) - 6:
            ready = min((w - WA + 1) // 2, windowed_gates + 2)
            plan += [("gate", i) for i in range(windowed_gates, ready)]
            windowed_gates = ready
    w_o = [("split", NT + e) for e in range(KD)]
    plan += [("load", n) for n in range(NT + 2, NT + KD)]
    plan += [w_o[0], ("values", steps - 2), w_o[1], ("msplit", 0), ("turns", steps - 1), ("msplit", 1), w_o[2]]
    plan += [("values", steps - 1), w_o[3], w_o[4]]
    plan += [("gate", i) for i in range(windowed_gates, NS)]
    plan += [("msplit", 2)] + w_o[5:]
    plan += [("out", 0, 2), ("result", 0), ("msplit", 3), ("result", 1), ("msplit", 4)]
    for i in range(2, NS):
        plan += [("out", i, 1), ("result", i)]
        plan += [("msplit", i + 3)] if i + 3 < NS else []
    return plan


PLAN = make_plan()


def build(nc, x, norm_w, w_in, sinks, lq1, lk1, lq2, lk2, subln_w, w_o, final_w, cos_t, sin_t, out):
    x_rows = x.rearrange("b (i p) d -> p (b i) d", p=P)
    out_rows = out.rearrange("b (i p) d -> p (b i) d", p=P)
    w_cols = w_in.rearrange("l (k p) c -> p (l k) c", p=P)

    with ExitStack() as ctx:
        def keep(name, shape, dt=F32):
            return ctx.enter_context(nc.sbuf_tensor(name, shape, dt))

        ident = keep("ident", [P, P])
        w_raw = keep("w_raw", [P, 2, KD, P])
        w_hi = keep("w_hi", [P, 2, KD, P], F32R)
        w_lo = keep("w_lo", [P, 2, KD, P], F32R)
        o_b = keep("o_b", [P, NB, NS, P])
        raw = keep("raw", [P, 2, HALF])
        swp = keep("swp", [P, 2, HALF])
        o_sq = keep("o_sq", [P, 4, P])
        minus_half = keep("minus_half", [P, 8])
        ss = keep("ss", [P, 6, 8])
        ms = keep("ms", [P, 6, 8])
        rstd = keep("rstd", [P, 6, 8])
        lam_in = keep("lam_in", [P, 4, HD])
        lam_s = keep("lam_s", [P, 8])
        lam_junk = keep("lam_junk", [P, 2, HD])
        neg_lam = keep("neg_lam", [P, 1])
        sub_w = keep("sub_w", [P, 1])
        sub_ws = keep("sub_ws", [P, 1])
        sink = keep("sink", [P, 8])
        neg_sink = keep("neg_sink", [P, 8])
        nmax = keep("nmax", [P, 2, 4])
        rsum = keep("rsum", [P, 2, 4])
        rinv = keep("rinv", [P, 2, 4])
        esink = keep("esink", [P, 2, 4])
        with ExitStack() as early:
            def first(name, shape, dt=F32):
                return early.enter_context(nc.sbuf_tensor(name, shape, dt))

            kb = first("kb", [P, 2, 2, S], F32R)
            qb = first("qb", [P, 2, 2, S], F32R)
            vb = first("vb", [P, 2, NS, P])
            qa = first("qa", [P, 4, S])
            va = first("va", [P, NS, P])
            pr = first("pr", [P, 2, S])
            at = first("at", [P, 2, S])
            aT = first("aT", [P, 2, HALF])
            cos = first("cos", [P, S])
            sin = first("sin", [P, S])
            xT_hi = first("xT_hi", [P, KD, S], F32R)
            xT_lo = first("xT_lo", [P, KD, S], F32R)
        with ExitStack() as tail:
            def last_of(name, shape, dt=F32):
                return tail.enter_context(nc.sbuf_tensor(name, shape, dt))

            ka = last_of("ka", [P, 2, S])
            _mix_place = last_of("mix_place", [P, 2, 2, KD, P])
            gA = last_of("gA", [P, 4, S])
            mixA = last_of("mixA", [P, 4, S])
            x_again = last_of("x_again", [P, 2, D])
            y = last_of("y", [P, 2, D])
            res = last_of("res", [P, 2, D])
            fin_w = last_of("fin_w", [P, D])
            _sin_place = last_of("sin_place", [P, D])
            wo_hi = last_of("wo_hi", [P, KD, D], F32R)
            with nc.sbuf_tensor("wo_in", [P, KD, D], F32) as wo_in:
                pass
            wo_lo = last_of("wo_lo", [P, KD, D], F32R)
        with ExitStack() as last:
            mix_parts = last.enter_context(nc.sbuf_tensor("mix_parts", [P, 3, 2, KD, P], F32R))
        x_low = o_b[:].rearrange("p h i e -> p (h i e)").rearrange("p (b d) -> p b d", d=D)

        def x_in(s, cols=slice(0, D)):
            return x_low[:, s, cols] if s < 4 else qa[:, s - 4, cols]

        mixB = o_b[:].rearrange("p h i e -> p h (i e)")
        norm_row = at[:, 1, :]
        at_a = at[:].rearrange("p b (h k) -> p b h k", h=4)
        pr_a = pr[:].rearrange("p b (h k) -> p b h k", h=4)

        def psum(name, shape):
            return ctx.enter_context(nc.psum_tensor(name, shape, F32))

        pS = psum("pS", [P, 2, 1024])
        pT = psum("pT", [P, 2, HALF])
        pO = psum("pO", [P, HALF])
        pP = psum("pP", [P, HALF])
        pS_a = pS[:].rearrange("p b (h k) -> p b h k", h=4)

        def sem(name):
            return ctx.enter_context(nc.semaphore(name))

        const_in = sem("const_in")
        norm_in = sem("norm_in")
        table_in = sem("table_in")
        x_in_s = [sem(f"x_in{s}") for s in range(NS)]
        const_ok = sem("const_ok")
        lam_dot = sem("lam_dot")
        lam_exp = sem("lam_exp")
        x_ss = sem("x_ss")
        x_rstd = sem("x_rstd")
        x_norm = sem("x_norm")
        turn_ok = sem("turn_ok")
        turn_act = sem("turn_act")
        turn_dve = sem("turn_dve")
        xhi_ok = sem("xhi_ok")
        w_in_s = [sem(f"w_in{b}") for b in range(2)]
        wo_in_s = [sem(f"wo_in{e}") for e in range(KD)]
        w_hi_ok = sem("w_hi_ok")
        w_lo_ok = sem("w_lo_ok")
        proj_ok = sem("proj_ok")
        copy_ok = sem("copy_ok")
        gate_ok = sem("gate_ok")
        swap_s = [sem(f"swap{b}") for b in range(2)]
        rope_mul = sem("rope_mul")
        rope_ok = sem("rope_ok")
        stack_hi = sem("stack_hi")
        stack_lo = sem("stack_lo")
        stack_s = [sem(f"stack{b}") for b in range(2)]
        ka_zero = sem("ka_zero")
        scores_ok = [sem(f"scores_ok{m}") for m in range(2)]
        max_ok = [sem(f"max_ok{m}") for m in range(2)]
        exp_ok = [sem(f"exp_ok{m}") for m in range(2)]
        esink_ok = sem("esink_ok")
        at_ok = sem("at_ok")
        av_ok = sem("av_ok")
        o_copied = sem("o_copied")
        o_ss = sem("o_ss")
        o_rstd = sem("o_rstd")
        o_norm = sem("o_norm")
        mixa_ok = sem("mixa_ok")
        mhi_ok = sem("mhi_ok")
        mlo_ok = sem("mlo_ok")
        out_ok = sem("out_ok")
        y_ok = sem("y_ok")
        y_ss = sem("y_ss")
        y_rstd = sem("y_rstd")
        res_ok = sem("res_ok")
        x_again_s = [sem(f"x_again{b}") for b in range(2)]
        fin_in = sem("fin_in")
        stored = [sem(f"stored{b}") for b in range(2)]
        dve_chain = sem("dve_chain")
        pool_chain = sem("pool_chain")

        projs = [st[1] for st in PLAN if st[0] == "copy"]
        kind_of = [TILES[t][0] for t, _ in projs]
        number = {ph: n for n, ph in enumerate(projs)}

        def count(n, kinds):
            return sum(k in kinds for k in kind_of[:n])

        ROTARY, VALUE, GATE = ("qa", "ka", "qb", "kb"), ("va", "vb"), ("ga", "gb")

        def bank_no(n):
            return n if n < PROLOGUE + 2 else PROLOGUE

        def bank(n):
            b = bank_no(n)
            return (pP, pO)[b - PROLOGUE][:, :] if b >= PROLOGUE else pS[:, b // 2, (b % 2) * HALF:(b % 2 + 1) * HALF]

        turns = []
        for st in PLAN:
            if st[0] == "xturn":
                turns += [("x", st[1], r) for r in range(2)]
            if st[0] == "place" and TILES[st[1][0]][0] in VALUE:
                turns.append(("v", st[1]))
            if st[0] == "place" and TILES[st[1][0]][0] == "gb":
                turns.append(("o", st[1]))
            if st[0] == "turns":
                w = st[1]
                n_turns = (w % NS + 4) // 4 if w < WA else (1 if w < WA + 2 else 2)
                turns += [("a", w, r) for r in range(n_turns)]
        turn_no = {t: n for n, t in enumerate(turns)}
        att_turns = [t for t in turns if t[0] == "a"]
        att_no = {t: n for n, t in enumerate(att_turns)}

        def turns_of(w):
            return [t for t in att_turns if t[1] == w]

        def turns_read(n, kinds):
            return sum(t[0] in kinds for t in turns[:n + 1])

        def wait_bank_free(pe, n):
            earlier = [j for j in range(n) if bank_no(j) == bank_no(n)]
            if earlier:
                pe.wait_ge(copy_ok, earlier[-1] + 1)
                if kind_of[earlier[-1]] in GATE:
                    pe.wait_ge(gate_ok, count(earlier[-1] + 1, GATE))

        def wait_stage_free(eng, n):
            if n < 2:
                return
            if kind_of[n - 2] == "gb":
                eng.wait_ge(turn_dve, turns_read(turn_no[("o", projs[n - 2])], ("x", "o")))
            elif kind_of[n - 2] == "ga":
                eng.wait_ge(gate_ok, count(n - 1, GATE))
            elif kind_of[n - 2] in VALUE:
                eng.wait_ge(turn_ok, turn_no[("v", projs[n - 2])] + 1)
            elif kind_of[n - 2] == "kb":
                eng.wait_ge(stack_s[n % 2], stacked(n - 2))
            elif kind_of[n - 2] == "qb":
                eng.wait_ge(stack_lo, count(n - 1, STACKED))
            else:
                eng.wait_ge(rope_ok, count(n - 1, ROTARY))

        def swaps(n):
            return 64 * sum(kind_of[j] in ROTARY for j in range(n % 2, n + 1, 2))

        def stacked(n):
            return 16 * sum({"kb": 2, "qb": 4}.get(kind_of[j], 0) for j in range(n % 2, n + 1, 2))

        def tile_done(kind, j, half=1):
            return number[(TILES.index((kind, j)), half)] + 1

        def o_visit(w):
            return w // 4 if w < WA else NS + w - WA

        def visit(w):
            return w if w < WA else WA + (w - WA) // 2

        def o_stat(stat, v):
            return stat[:, 2 + v // 2, 4 * (v % 2):4 * (v % 2) + 4]

        def stack_places(half):
            (kind, j), frames, n = TILES[half[0]], slice(half[1] * HALF, (half[1] + 1) * HALF), number[half]
            for m in range(2):
                rows = slice(m * HD, (m + 1) * HD)
                if kind == "kb":
                    yield rows, kb[rows, j % 2, m, frames], raw[rows, n % 2, :].bitcast(F32R)
                else:
                    yield rows, qb[rows, 0, m, frames], qb[rows, 1, m, frames]

        def wo_raw(e):
            return w_raw[:, (NT + e) % 2].rearrange("p k c -> p (k c)") if e < 2 else wo_in[:, e, :]

        def mix_part(i):
            return (i + 1) % 3

        def out_banks(i):
            return pT[:].rearrange("p b c -> p (b c)") if i % 3 == 2 else pS[:, i % 3, :]

        def result_parts(i):
            return [slice(0, HALF), slice(HALF, D)] if i == NS - 1 else [slice(0, D)]

        def columns_a(i):
            return (P, P) if i == 0 else (CHUNK, P + CHUNK)

        block = ctx.enter_context(nc.Block())

        @block.sync
        def _(sp):
            def load_w(n):
                if n == NT + 2:
                    sp.wait_ge(proj_ok, len(projs))
                if 2 <= n < NT + 2:
                    sp.wait_ge(w_hi_ok, n - 1)
                    sp.wait_ge(w_lo_ok, n - 1)
                b = n % 2
                if n >= NT:
                    e = n - NT
                    dst = wo_raw(e)
                    for g in range(2):
                        r = g * 4 * HD + e * HD if e < 4 else e * P + g * HD
                        sp.dma_start(dst[g * HD:(g + 1) * HD], w_o[0, r:r + HD, :]).then_inc(wo_in_s[e], 16)
                    return
                kind, j = TILES[n]
                for g in range(2):
                    if kind in ("qa", "ga"):
                        c = COLUMNS[kind] + g * 4 * HD + j * HD
                        sp.dma_start(w_raw[:, b, :, g * HD:(g + 1) * HD], w_cols[:, :, c:c + HD]).then_inc(w_in_s[b], 16)
                    else:
                        c = COLUMNS[kind] + j * P
                        k = slice(g * KD // 2, (g + 1) * KD // 2)
                        sp.dma_start(w_raw[:, b, k, :], w_cols[:, k, c:c + P]).then_inc(w_in_s[b], 16)

            def load_x(s):
                sp.dma_start(x_in(s), x_rows[:, s, :]).then_inc(x_in_s[s], 16)

            load_x(0)
            sp.dma_start(norm_row, norm_w[0:1, :].broadcast_to([P, D])).then_inc(norm_in, 16)
            for s in range(1, 4):
                load_x(s)
            load_w(0)
            load_x(4)
            load_w(1)
            for s in range(5, NS):
                load_x(s)
            sp.dma_start(cos[:], cos_t).then_inc(table_in, 16)
            sp.dma_start(sin[:], sin_t).then_inc(table_in, 16)
            for dst, src in ((lam_in[:, 0], lq1[0:1, :].broadcast_to([P, HD])),
                             (lam_in[:, 1], lk1[0:1, :].broadcast_to([P, HD])),
                             (lam_in[:, 2], lq2[0:1, :].broadcast_to([P, HD])),
                             (lam_in[:, 3], lk2[0:1, :].broadcast_to([P, HD])),
                             (sub_w[:], subln_w.rearrange("l e -> e l")),
                             (sink[:], sinks[0:1, :].broadcast_to([P, 8]))):
                sp.dma_start(dst, src).then_inc(const_in, 16)
            for st in PLAN:
                if st[0] == "load":
                    load_w(st[1])
                if st[0] == "copy" and TILES[st[1][0]][0] in ROTARY:
                    n = number[st[1]]
                    sp.wait_ge(copy_ok, n + 1)
                    for q in range(4):
                        to, fr = 32 * q, 32 * (q ^ 1)
                        sp.dma_start(swp[to:to + 32, n % 2, :], raw[fr:fr + 32, n % 2, :]).then_inc(swap_s[n % 2], 16)
                if st[0] == "stack":
                    (t, half), n = st[1], number[st[1]]
                    kind, j = TILES[t]
                    frames = slice(half * HALF, (half + 1) * HALF)
                    low, high = slice(0, HD), slice(HD, P)
                    sp.wait_ge(stack_lo, count(n + 1, STACKED))
                    if kind == "kb":
                        k, lo = kb[:, j % 2].bitcast(F32), raw[:, n % 2, :]
                        copies = [(k[high, 0, frames], lo[low]), (k[low, 1, frames], lo[high])]
                    else:
                        q = qb[:].bitcast(F32)
                        copies = [(q[high, 1 - v, 0, frames], q[low, v, 0, frames]) for v in range(2)]
                        copies += [(q[low, 1 - v, 1, frames], q[high, v, 1, frames]) for v in range(2)]
                    for dst, src in copies:
                        sp.dma_start(dst, src).then_inc(stack_s[n % 2], 16)
                if st == ("msplit", 0):
                    sp.wait_ge(rope_ok, count(len(projs), ROTARY))
                    sp.dma_start(fin_w[:], final_w.rearrange("(o d) -> o d", o=1).broadcast_to([P, D])).then_inc(fin_in, 16)
                    sp.wait_ge(av_ok, len(att_turns))
                    for b in range(2):
                        sp.dma_start(x_again[:, b, :], x_rows[:, b, :]).then_inc(x_again_s[b], 16)
                if st[0] == "result":
                    i = st[1]
                    for p, cols in enumerate(result_parts(i)):
                        sp.wait_ge(res_ok, i + p + 1)
                        sp.dma_start(out_rows[:, i, cols], res[:, i % 2, cols]).then_inc(stored[i % 2], 16)
                    if i + 2 < NS:
                        sp.dma_start(x_again[:, i % 2, :], x_rows[:, i + 2, :]).then_inc(x_again_s[i % 2], 16)
            for b in range(2):
                sp.wait_ge(stored[b], 16 * (NS // 2 + b))

        @block.tensor
        def _(pe):
            def turn(t, blocks):
                n = turn_no[t]
                if n >= 2 and turns[n - 2][0] in ("x", "o"):
                    pe.wait_ge(turn_dve, turns_read(n - 2, ("x", "o")))
                elif n >= 2:
                    pe.wait_ge(turn_act, turns_read(n - 2, ("a", "v")))
                for k, src in enumerate(blocks):
                    tr = pe.transpose(pT[:, n % 2, k * P:(k + 1) * P], src, ident[:])
                tr.then_inc(turn_ok, 1)

            pe.wait_ge(const_ok, 1)
            for st in PLAN:
                if st[0] == "xturn":
                    s = st[1]
                    pe.wait_ge(x_norm, s + 1)
                    for r in range(2):
                        turn(("x", s, r), [x_in(s, slice((4 * r + k) * P, (4 * r + k + 1) * P)) for k in range(4)])
                if st[0] == "proj":
                    (t, half), a, b = st[1:]
                    n = number[st[1]]
                    if a == 0:
                        if half == 0:
                            pe.wait_ge(w_hi_ok, t + 1)
                            pe.wait_ge(w_lo_ok, t + 1)
                        if t == 0:
                            pe.wait_ge(turn_dve, NS * (half + 1))
                        wait_bank_free(pe, n)
                    frames = slice(half * HALF, (half + 1) * HALF)
                    for q in range(a, b):
                        k, part = q // 3, q % 3
                        w = (w_hi, w_hi, w_lo)[part][:, t % 2, k, :]
                        xt = (xT_hi, xT_lo, xT_hi)[part][:, k, frames]
                        mm = pe.matmul(bank(n), w, xt, start=(q == 0), stop=(q == 3 * KD - 1))
                    if b == 3 * KD:
                        mm.then_inc(proj_ok, 1)
                if st[0] == "place" and TILES[st[1][0]][0] in VALUE:
                    n = number[st[1]]
                    pe.wait_ge(copy_ok, n + 1)
                    turn(("v", st[1]), [raw[:, n % 2, k * P:(k + 1) * P] for k in range(4)])
                if st[0] == "place" and TILES[st[1][0]][0] == "gb":
                    t, half = st[1]
                    h = TILES[t][1]
                    pe.wait_ge(o_norm, 2 * h + half + 1)
                    turn(("o", st[1]), [o_b[:, h, 4 * half + k, :] for k in range(4)])
                if st[0] == "scores" and st[1] < WA:
                    w, m = st[1:]
                    h, i = w // NS, w % NS
                    if i in (0, NS // 2) and m == 0:
                        for kind in ("kb", "qb"):
                            n = tile_done(kind, h, 2 * i // NS) - 1
                            pe.wait_ge(stack_s[n % 2], stacked(n))
                    if w == 0:
                        pe.wait_ge(copy_ok, PROLOGUE)
                    else:
                        pe.wait_ge(exp_ok[m], w)
                    keys = (i + 1) * P
                    for c in range(0, keys, HALF):
                        e = min(keys, c + HALF)
                        for v in range(2):
                            mm = pe.matmul(pS[:, m, c:e], qb[:, v, m, i * P:(i + 1) * P], kb[:, h % 2, m, c:e],
                                           start=(v == 0), stop=(v == 1))
                    mm.then_inc(scores_ok[m], 1)
                if st[0] == "scores" and st[1] >= WA:
                    w, m = st[1:]
                    i = (w - WA) // 2
                    if i == 0:
                        pe.wait_ge(rope_ok, count(tile_done("ka", 0), ROTARY))
                    pe.wait_ge(exp_ok[m], visit(w))
                    c, nk = columns_a(i)
                    for t in range(4):
                        mm = pe.matmul(pS_a[:, m, t, c:c + nk], qa[:, t, i * P:(i + 1) * P],
                                       ka[:, m, (i + 1) * P - nk:(i + 1) * P], start=True, stop=True)
                    mm.then_inc(scores_ok[m], 1)
                if st[0] == "turns":
                    w = st[1]
                    pe.wait_ge(at_ok, w + 1)
                    for t in turns_of(w):
                        if w < WA:
                            turn(t, [at[:, w % 2, k * P:(k + 1) * P]
                                     for k in range(4 * t[2], min(4 * t[2] + 4, w % NS + 1))])
                        else:
                            c = (t[2] if w >= WA + 2 else 1) * P
                            turn(t, [at_a[:, w % 2, hh, c:c + P] for hh in range(4)])
                if st[0] == "values":
                    w = st[1]
                    if w == 0:
                        pe.wait_ge(copy_ok, PROLOGUE + 2)
                    if o_visit(w) >= 1 and (w >= WA or w % 4 == 0):
                        pe.wait_ge(o_copied, o_visit(w))
                    for t in turns_of(w):
                        pe.wait_ge(turn_act, turns_read(turn_no[t], ("a", "v")))
                        src = aT[:, att_no[t] % 2, :]
                        if w < WA:
                            h, i = w // NS, w % NS
                            if i in (0, 4) and t[2] == 0:
                                v = ("v", (TILES.index(("vb", h)), i // 4))
                                pe.wait_ge(turn_act, turns_read(turn_no[v], ("a", "v")))
                            for k in range(4 * t[2], min(4 * t[2] + 4, i + 1)):
                                mm = pe.matmul(pO[:, (i % 4) * P:(i % 4 + 1) * P], src[:, (k % 4) * P:(k % 4 + 1) * P],
                                               vb[:, h % 2, k, :], start=(k == 0), stop=(k == i))
                        else:
                            i = (w - WA) // 2
                            if i == 0:
                                v = ("v", (TILES.index(("va", 0)), 1))
                                pe.wait_ge(turn_act, turns_read(turn_no[v], ("a", "v")))
                            k = i - len(turns_of(w)) + 1 + t[2]
                            mm = pe.matmul(pO[:, :], va[:, k, :], src, start=(t is turns_of(w)[0]),
                                           stop=(t is turns_of(w)[-1]))
                        mm.then_inc(av_ok, 1)
                if st[0] == "out":
                    blocks = range(st[1], st[1] + st[2])
                    for i in blocks:
                        if i < 2:
                            pe.wait_ge(exp_ok[i], WA + NS)
                        elif i == 2:
                            pe.wait_ge(turn_act, turns_read(len(turns) - 1, ("a", "v")))
                            pe.wait_ge(turn_dve, turns_read(len(turns) - 1, ("x", "o")))
                        else:
                            pe.wait_ge(y_ok, i - 2)
                        pe.wait_ge(mlo_ok, i + 1)
                    for c0 in ((0, 1) if NS - 1 in blocks else (None,)):
                        for k in range(KD):
                            if st[1] == 0:
                                pe.wait_ge(w_hi_ok, NT + k + 1)
                                pe.wait_ge(w_lo_ok, NT + k + 1)
                            for i in blocks:
                                mix_hi, mix_lo = (mix_parts[:, mix_part(i), part, k, :] for part in range(2))
                                for c in ((0, 1) if c0 is None else (c0,)):
                                    cols = slice(c * HALF, (c + 1) * HALF)
                                    for q, (mix, wo) in enumerate(((mix_hi, wo_hi), (mix_hi, wo_lo), (mix_lo, wo_hi))):
                                        mm = pe.matmul(out_banks(i)[:, cols], mix, wo[:, k, cols],
                                                       start=(k == 0 and q == 0), stop=(k == KD - 1 and q == 2))
                                if k == KD - 1:
                                    mm.then_inc(out_ok, 1)

        @block.scalar
        def _(act):
            def copy(out_, in_, scale=1.0):
                return nc.scalar.activation(out_, in_, ACT.Copy, scale=scale)

            for st in PLAN:
                if st[0] == "lambda":
                    act.wait_ge(lam_dot, 2)
                    nc.scalar.activation(lam_s[:, 2:4], lam_s[:, 0:2], ACT.Exp).then_inc(lam_exp, 1)
                if st[0] == "xsquare":
                    s = st[1]
                    act.wait_ge(x_in_s[s], 16)
                    if s:
                        act.wait_ge(x_ss, s)
                    nc.scalar.activation(pr[:, 0, :], x_in(s), ACT.Square,
                                         accum_out=ss[:, 0, s:s + 1]).then_inc(x_ss, 1)
                if st[0] == "xturn":
                    s = st[1]
                    for r in range(2):
                        n = turn_no[("x", s, r)]
                        act.wait_ge(turn_ok, n + 1)
                        copy(xT_hi[:, 4 * r:4 * r + 4, s * P:(s + 1) * P],
                             pT[:, n % 2, :].rearrange("p (k s) -> p k s", k=4)).then_inc(xhi_ok, 1)
                if st[0] == "split":
                    n = st[1]
                    if n < NT:
                        act.wait_ge(w_in_s[n % 2], 32 * (n // 2 + 1))
                        if n >= 2:
                            act.wait_ge(proj_ok, number[(n - 2, 1)] + 1)
                        copy(w_hi[:, n % 2], w_raw[:, n % 2]).then_inc(w_hi_ok, 1)
                    else:
                        act.wait_ge(wo_in_s[n - NT], 32)
                        if n == NT:
                            act.wait_ge(proj_ok, len(projs))
                        copy(wo_hi[:, n - NT, :], wo_raw(n - NT)).then_inc(w_hi_ok, 1)
                if st[0] == "copy":
                    n = number[st[1]]
                    act.wait_ge(proj_ok, n + 1)
                    wait_stage_free(act, n)
                    if kind_of[n] in GATE:
                        nc.scalar.activation(raw[:, n % 2, :], bank(n), ACT.Tanh, scale=0.5).then_inc(copy_ok, 1)
                    else:
                        copy(raw[:, n % 2, :], bank(n), SCALE if kind_of[n][0] == "q" else 1.0).then_inc(copy_ok, 1)
                if st[0] == "stack":
                    n = number[st[1]]
                    act.wait_ge(rope_ok, count(n + 1, ROTARY))
                    kind, j = TILES[st[1][0]]
                    if kind == "kb" and j >= 2:
                        for m in range(2):
                            act.wait_ge(scores_ok[m], NS * (j - 1))
                    if kind == "qb" and j >= 1:
                        for m in range(2):
                            act.wait_ge(scores_ok[m], NS * (j - 1) + 4 * (st[1][1] + 1))
                    for rows, hi, lo in stack_places(st[1]):
                        ins = copy(hi, raw[rows, n % 2, :])
                    ins.then_inc(stack_hi, 1)
                if st[0] == "place" and TILES[st[1][0]][0] in VALUE:
                    n = turn_no[("v", st[1])]
                    (t, half), j = st[1], TILES[st[1][0]][1]
                    act.wait_ge(turn_ok, n + 1)
                    if TILES[t][0] == "vb":
                        if j >= 2:
                            act.wait_ge(av_ok, sum(x_[1] < NS * (j - 1) for x_ in att_turns))
                        dst = vb[:, j % 2, 4 * half:4 * half + 4, :]
                    else:
                        dst = va[:, 4 * half:4 * half + 4, :]
                    copy(dst, pT[:, n % 2, :].rearrange("p (k s) -> p k s", k=4)).then_inc(turn_act, 1)
                if st[0] == "softmax":
                    w = st[1]
                    if w < WA:
                        keys = (w % NS + 1) * P
                        if w >= 1:
                            act.wait_ge(at_ok, w)
                        for m in range(2):
                            act.wait_ge(max_ok[m], w + 1)
                            nc.scalar.activation(pr[:, m, 0:keys], pS[:, m, 0:keys], ACT.Exp, bias=nmax[:, m, 0:1],
                                                 accum_out=rsum[:, m, 0:1]).then_inc(exp_ok[m], 1)
                    else:
                        m, i = w % 2, (w - WA) // 2
                        c, nk = columns_a(i)
                        act.wait_ge(at_ok, w if w < WA + 1 else w - 1)
                        act.wait_ge(max_ok[m], visit(w) + 1)
                        for t in range(4):
                            e = nc.scalar.activation(pr_a[:, m, t, c:c + nk], pS_a[:, m, t, c:c + nk], ACT.Exp,
                                                     bias=nmax[:, m, t:t + 1], accum_out=rsum[:, m, t:t + 1])
                        e.then_inc(exp_ok[m], 1)
                        nc.scalar.activation(esink[:, 1, :], esink[:, 0, :], ACT.Exp).then_inc(esink_ok, 1)
                if st[0] == "turns":
                    for t in turns_of(st[1]):
                        n, a = turn_no[t], att_no[t]
                        act.wait_ge(turn_ok, n + 1)
                        if a >= 2:
                            act.wait_ge(av_ok, a - 1)
                        width = P * min(4, st[1] % NS + 1 - 4 * t[2]) if st[1] < WA else HALF
                        copy(aT[:, a % 2, 0:width], pT[:, n % 2, 0:width]).then_inc(turn_act, 1)
                if st[0] == "values":
                    w = st[1]
                    if w >= WA or w % 4 == 3:
                        act.wait_ge(av_ok, att_no[turns_of(w)[-1]] + 1)
                    if w < WA and w % 4 == 3:
                        h, i = w // NS, w % NS
                        if w >= 7:
                            act.wait_ge(o_ss, w // 4)
                        nc.scalar.activation(o_sq[:], pO[:].rearrange("p (k e) -> p k e", k=4), ACT.Square)
                        copy(o_b[:, h, i - 3:i + 1, :], pO[:].rearrange("p (k e) -> p k e", k=4)).then_inc(o_copied, 1)
                    if w >= WA:
                        i, r = (w - WA) // 2, slice((w % 2) * HD, (w % 2 + 1) * HD)
                        copy(mixA[r, :, i * P:(i + 1) * P], pO[r, :].rearrange("p (k e) -> p k e", k=4)).then_inc(o_copied, 1)
                if st[0] == "msplit":
                    i = st[1]
                    if i == 2:
                        for m in range(2):
                            act.wait_ge(scores_ok[m], WA + NS)
                    if i == 0:
                        act.wait_ge(turn_dve, turns_read(len(turns) - 1, ("x", "o")))
                    act.wait_ge(mixa_ok, i + 1)
                    if i >= 3:
                        act.wait_ge(out_ok, i - 2)
                    copy(mix_parts[:, mix_part(i), 0, 0:4, :], mixA[:, :, i * P:(i + 1) * P])
                    copy(mix_parts[:, mix_part(i), 0, 4:8, :], mixB[:, :, i * P:(i + 1) * P]).then_inc(mhi_ok, 1)
                if st[0] == "result":
                    i = st[1]
                    if i >= 2:
                        act.wait_ge(stored[i % 2], 16 * (i // 2))
                    for p, cols in enumerate(result_parts(i)):
                        act.wait_ge(y_ok, i + p + 1)
                        nc.scalar.activation(res[:, i % 2, cols], y[:, i % 2, cols], ACT.Square,
                                             accum_out=ss[:, 1 - p, i:i + 1]).then_inc(y_ss, 1)

        @block.vector
        def _(dve):
            chain = [0]

            def link(ins):
                chain[0] += 1
                ins.then_inc(dve_chain, 1)
                dve.wait_ge(dve_chain, chain[0])

            for st in PLAN:
                if st[0] == "lambda":
                    dve.wait_ge(const_in, 16 * 6)
                    for j in range(2):
                        nc.vector.tensor_tensor_reduce(out=lam_junk[:, j], in0=lam_in[:, 2 * j], in1=lam_in[:, 2 * j + 1], scale=1.0,
                                                       scalar=0.0, op0=ALU.mult, op1=ALU.add,
                                                       accum_out=lam_s[:, j:j + 1]).then_inc(lam_dot, 1)
                    link(nc.vector.tensor_scalar(neg_sink[:], sink[:], -1.0, None, ALU.mult))
                    link(nc.vector.tensor_scalar(sub_ws[:], sub_w[:], (1.0 - LAMBDA_INIT) * 0.5, None, ALU.mult))
                    dve.wait_ge(lam_exp, 1)
                    link(nc.vector.tensor_tensor(lam_s[:, 4:5], lam_s[:, 2:3], lam_s[:, 3:4], ALU.subtract))
                    link(nc.vector.tensor_scalar(neg_lam[:], lam_s[:, 4:5], -1.0, -LAMBDA_INIT, ALU.mult, ALU.add))
                if st[0] == "xnorm":
                    s = st[1]
                    if s == 0:
                        dve.wait_ge(norm_in, 16)
                    dve.wait_ge(x_rstd, s + 1)
                    nc.vector.scalar_tensor_tensor(out=x_in(s), in0=x_in(s), scalar=rstd[:, 0, s:s + 1],
                                                   in1=norm_row, op0=ALU.mult, op1=ALU.mult).then_inc(x_norm, 1)
                if st[0] == "xturn":
                    s = st[1]
                    for r in range(2):
                        n = turn_no[("x", s, r)]
                        dve.wait_ge(xhi_ok, 2 * s + r + 1)
                        hi = xT_hi[:, 4 * r:4 * r + 4, s * P:(s + 1) * P]
                        nc.vector.tensor_tensor(xT_lo[:, 4 * r:4 * r + 4, s * P:(s + 1) * P],
                                                pT[:, n % 2, :].rearrange("p (k s) -> p k s", k=4),
                                                hi.bitcast(F32), ALU.subtract).then_inc(turn_dve, 1)
                if st[0] == "split" and st[1] in DVE_SPLITS:
                    n = st[1]
                    dve.wait_ge(w_hi_ok, n + 1)
                    nc.vector.tensor_tensor(w_lo[:, n % 2], w_raw[:, n % 2], w_hi[:, n % 2].bitcast(F32),
                                            ALU.subtract).then_inc(w_lo_ok, 1)
                if st[0] == "copy" and TILES[st[1][0]][0] in GATE:
                    n = number[st[1]]
                    dve.wait_ge(copy_ok, n + 1)
                    (t, half), j = st[1], TILES[st[1][0]][1]
                    if TILES[t][0] == "ga":
                        dve.wait_ge(av_ok, sum(x_[1] < WA for x_ in att_turns))
                        dst = gA[:, j, half * HALF:(half + 1) * HALF]
                    else:
                        dst = swp[:, n % 2, :]
                    nc.vector.scalar_tensor_tensor(out=dst, in0=raw[:, n % 2, :], scalar=1.0, in1=bank(n),
                                                   op0=ALU.add, op1=ALU.mult).then_inc(gate_ok, 1)
                if st[0] == "place":
                    (t, half), n = st[1], number[st[1]]
                    kind, j = TILES[t]
                    frames = slice(half * HALF, (half + 1) * HALF)
                    if kind in ROTARY:
                        if n == 0:
                            dve.wait_ge(table_in, 32)
                        dve.wait_ge(swap_s[n % 2], swaps(n))
                        link(nc.vector.tensor_tensor(raw[:, n % 2, :], raw[:, n % 2, :], cos[:, frames], ALU.mult))
                        dve.wait_ge(rope_mul, count(n + 1, ROTARY))
                        if kind in STACKED:
                            places = [(slice(0, P), raw[:, n % 2, :])]
                        elif kind == "qa":
                            places = [(slice(0, P), qa[:, j, frames])]
                        else:
                            half_rows = [slice(m * HD, (m + 1) * HD) for m in range(2)]
                            places = [(r, ka[r, m, frames]) for m, r in enumerate(half_rows)]
                            dve.wait_ge(ka_zero, 1)
                        for rows, dst in places:
                            sum_ = nc.vector.tensor_tensor(dst, raw[rows, n % 2, :], swp[rows, n % 2, :], ALU.add)
                        sum_.then_inc(rope_ok, 1)
                    if kind == "gb":
                        tn = turn_no[("o", st[1])]
                        dve.wait_ge(turn_ok, tn + 1)
                        dve.wait_ge(gate_ok, count(n + 1, GATE))
                        nc.vector.scalar_tensor_tensor(out=mixB[:, j, frames], in0=pT[:, tn % 2, :], scalar=sub_ws[:, 0:1],
                                                       in1=swp[:, n % 2, :], op0=ALU.mult,
                                                       op1=ALU.mult).then_inc(turn_dve, 1)
                if st[0] == "stack":
                    n = number[st[1]]
                    dve.wait_ge(stack_hi, count(n + 1, STACKED))
                    for rows, hi, lo in stack_places(st[1]):
                        ins = nc.vector.tensor_tensor(lo, raw[rows, n % 2, :], hi.bitcast(F32), ALU.subtract)
                    ins.then_inc(stack_lo, 1)
                if st[0] == "gate":
                    i = st[1]
                    dve.wait_ge(o_copied, NS + 2 * i + 2)
                    dve.wait_ge(gate_ok, count(tile_done("ga", 3), GATE))
                    rows = mixA[:, :, i * P:(i + 1) * P]
                    nc.vector.scalar_tensor_tensor(out=rows, in0=rows, scalar=0.5, in1=gA[:, :, i * P:(i + 1) * P],
                                                   op0=ALU.mult, op1=ALU.mult).then_inc(mixa_ok, 1)
                if st[0] == "softmax" and st[1] < WA:
                    w = st[1]
                    keys = (w % NS + 1) * P
                    for m in range(2):
                        dve.wait_ge(scores_ok[m], w + 1)
                        link(nc.vector.memset(pS[0:CHUNK, m, keys - CHUNK:keys], NEG))
                        nc.vector.tensor_reduce(nmax[:, m, 0:1], pS[:, m, 0:keys], AX_X, ALU.max,
                                                negate=True).then_inc(max_ok[m], 1)
                    for m in range(2):
                        dve.wait_ge(exp_ok[m], w + 1)
                    link(nc.vector.reciprocal(rinv[:, :, 0:1], rsum[:, :, 0:1]))
                    link(nc.vector.tensor_scalar(rinv[:, 1, 1:2], rinv[:, 1, 0:1], neg_lam[:, 0:1], None, ALU.mult))
                    link(nc.vector.tensor_scalar(pr[:, 1, 0:keys], pr[:, 1, 0:keys], rinv[:, 1, 1:2], None, ALU.mult))
                    if w >= 2:
                        dve.wait_ge(turn_ok, turn_no[turns_of(w - 2)[-1]] + 1)
                    nc.vector.scalar_tensor_tensor(out=at[:, w % 2, 0:keys], in0=pr[:, 0, 0:keys], scalar=rinv[:, 0, 0:1],
                                                   in1=pr[:, 1, 0:keys], op0=ALU.mult, op1=ALU.add).then_inc(at_ok, 1)
                if st[0] == "softmax" and st[1] >= WA:
                    w = st[1]
                    m, i = w % 2, (w - WA) // 2
                    c, nk = columns_a(i)
                    dve.wait_ge(scores_ok[m], visit(w) + 1)
                    link(nc.vector.memset(pS_a[0:CHUNK, m, :, 3 * CHUNK:4 * CHUNK], NEG))
                    if i > 0:
                        link(nc.vector.memset(pS_a[CHUNK:P, m, :, CHUNK:2 * CHUNK], NEG))
                    link(nc.vector.tensor_reduce(nmax[:, m, :], pS_a[:, m, :, c:c + nk], AX_X, ALU.max, negate=True))
                    link(nc.vector.tensor_tensor(nmax[:, m, :], nmax[:, m, :], neg_sink[:, 4 * m:4 * m + 4], ALU.min))
                    nc.vector.tensor_tensor(esink[:, 0, :], nmax[:, m, :], neg_sink[:, 4 * m:4 * m + 4],
                                            ALU.subtract).then_inc(max_ok[m], 1)
                    dve.wait_ge(exp_ok[m], visit(w) + 1)
                    dve.wait_ge(esink_ok, w - WA + 1)
                    link(nc.vector.tensor_tensor(rsum[:, m, :], rsum[:, m, :], esink[:, 1, :], ALU.add))
                    link(nc.vector.reciprocal(rinv[:, m, :], rsum[:, m, :]))
                    dve.wait_ge(turn_ok, turn_no[turns_of(w - 2)[-1]] + 1)
                    if w < WA + 2:
                        nc.vector.memset(at_a[:, m, :, 0:CHUNK], 0.0)
                    nc.vector.tensor_tensor(at_a[:, m, :, c:c + nk], pr_a[:, m, :, c:c + nk],
                                            rinv[:, m, :].unsqueeze(2).broadcast_to([P, 4, nk]), ALU.mult).then_inc(at_ok, 1)
                if st[0] == "values" and st[1] < WA and st[1] % 4 == 3:
                    v = o_visit(st[1])
                    dve.wait_ge(o_copied, v + 1)
                    nc.vector.tensor_reduce(o_stat(ss, v), o_sq[:], AX_X, ALU.add).then_inc(o_ss, 1)
                if st[0] == "values" and st[1] % 4 == 0 and 4 <= st[1] <= WA:
                    v = o_visit(st[1]) - 1 if st[1] < WA else NS - 1
                    dve.wait_ge(o_rstd, v + 1)
                    rows = o_b[:, v // 2, 4 * (v % 2):4 * (v % 2) + 4, :]
                    nc.vector.tensor_tensor(rows, rows, o_stat(rstd, v).unsqueeze(2).broadcast_to([P, 4, P]),
                                            ALU.mult).then_inc(o_norm, 1)
                if st[0] == "msplit":
                    i = st[1]
                    dve.wait_ge(mhi_ok, i + 1)
                    for g, mix in enumerate((mixA, mixB)):
                        hi, lo_ = (mix_parts[:, mix_part(i), part, 4 * g:4 * g + 4, :] for part in range(2))
                        lo = nc.vector.tensor_tensor(lo_, mix[:, :, i * P:(i + 1) * P], hi.bitcast(F32), ALU.subtract)
                    lo.then_inc(mlo_ok, 1)
                if st[0] == "result":
                    i = st[1]
                    b = i % 2
                    if i == 0:
                        dve.wait_ge(fin_in, 16)
                    dve.wait_ge(x_again_s[b], 16 * (i // 2 + 1))
                    for p, cols in enumerate(result_parts(i)):
                        dve.wait_ge(out_ok, i + p + 1)
                        nc.vector.tensor_tensor(y[:, b, cols], out_banks(i)[:, cols], x_again[:, b, cols],
                                                ALU.add).then_inc(y_ok, 1)
                    dve.wait_ge(y_rstd, i + 1)
                    for cols in result_parts(i):
                        nc.vector.scalar_tensor_tensor(out=res[:, b, cols], in0=y[:, b, cols], scalar=rstd[:, 1, i:i + 1],
                                                       in1=fin_w[:, cols], op0=ALU.mult, op1=ALU.mult).then_inc(res_ok, 1)

        @block.gpsimd
        def _(pool):
            chain = [0]

            def link(ins):
                chain[0] += 1
                ins.then_inc(pool_chain, 1)
                pool.wait_ge(pool_chain, chain[0])

            def inverse_root(stat, sums, scale, eps, done):
                mean, root = stat
                link(nc.gpsimd.tensor_scalar(mean, sums, scale, eps, ALU.mult, ALU.add))
                nc.gpsimd.tensor_tensor(root, mean, minus_half[:, 0:root.shape[1]], ALU.pow).then_inc(done, 1)

            link(nc.gpsimd.memset(minus_half[:], -0.5))
            link(nc.gpsimd.memset(ident[:], 0.0))
            nc.gpsimd.affine_select(out=ident[:], in_=ident[:], compare_op=ALU.not_equal, fill=1.0, base=0,
                                    pattern=[[-1, P]], channel_multiplier=1).then_inc(const_ok, 1)
            for st in PLAN:
                if st[0] == "xroot":
                    s = st[1]
                    pool.wait_ge(x_ss, s + 1)
                    inverse_root((ms[:, 0, s:s + 1], rstd[:, 0, s:s + 1]), ss[:, 0, s:s + 1], 1.0 / D, NORM_EPS, x_rstd)
                if st[0] == "split" and st[1] < NT and st[1] not in DVE_SPLITS:
                    n = st[1]
                    pool.wait_ge(w_hi_ok, n + 1)
                    nc.gpsimd.tensor_tensor(w_lo[:, n % 2], w_raw[:, n % 2], w_hi[:, n % 2].bitcast(F32),
                                            ALU.subtract).then_inc(w_lo_ok, 1)
                if st[0] == "split" and st[1] >= NT:
                    n = st[1]
                    pool.wait_ge(w_hi_ok, n + 1)
                    nc.gpsimd.tensor_tensor(wo_lo[:, n - NT, :], wo_raw(n - NT),
                                            wo_hi[:, n - NT, :].bitcast(F32), ALU.subtract).then_inc(w_lo_ok, 1)
                if st[0] == "copy" and TILES[st[1][0]][0] in ROTARY:
                    n = number[st[1]]
                    half = st[1][1]
                    frames = slice(half * HALF, (half + 1) * HALF)
                    if n == 0:
                        pool.wait_ge(table_in, 32)
                    pool.wait_ge(swap_s[n % 2], swaps(n))
                    nc.gpsimd.tensor_tensor(swp[:, n % 2, :], swp[:, n % 2, :], sin[:, frames],
                                            ALU.mult).then_inc(rope_mul, 1)
                if st == ("values", 3 * NS - 1):
                    for m in range(2):
                        pool.wait_ge(scores_ok[m], 3 * NS)
                    nc.gpsimd.memset(ka[:], 0.0).then_inc(ka_zero, 1)
                if st[0] == "values" and st[1] < WA and st[1] % 4 == 3:
                    v = o_visit(st[1])
                    pool.wait_ge(o_ss, v + 1)
                    inverse_root((o_stat(ms, v), o_stat(rstd, v)), o_stat(ss, v), 1.0 / P, SUBLN_EPS, o_rstd)
                if st[0] == "result":
                    i = st[1]
                    pool.wait_ge(y_ss, i + len(result_parts(i)))
                    if len(result_parts(i)) == 2:
                        link(nc.gpsimd.tensor_tensor(ss[:, 1, i:i + 1], ss[:, 1, i:i + 1], ss[:, 0, i:i + 1], ALU.add))
                    inverse_root((ms[:, 1, i:i + 1], rstd[:, 1, i:i + 1]), ss[:, 1, i:i + 1], 1.0 / D, NORM_EPS, y_rstd)


def rotary_tables():
    inv_freq = (1.0 / (np.float32(10000.0) ** (np.arange(0, HD, 2, dtype=np.float32) / np.float32(HD)))).astype(np.float32)
    freqs = np.arange(S, dtype=np.float32)[None, :] * inv_freq[:, None]
    c, s = np.cos(freqs.astype(np.float64)), np.sin(freqs.astype(np.float64))
    return (np.concatenate([c, c] * 2).astype(np.float32), np.concatenate([-s, s] * 2).astype(np.float32))


_INS = ["x", "norm_w", "w_in", "sinks", "lambda_q1", "lambda_k1", "lambda_q2", "lambda_k2", "subln_w", "w_o",
        "final_norm_w"]


def kernel(**inputs):
    import concourse.bacc as bacc
    from concourse.bass_utils import run_bass_kernel_spmd

    nc = bacc.Bacc("TRN2", target_bir_lowering=False, num_devices=1)
    arrays, args = {}, []
    cos_t, sin_t = rotary_tables()
    for name, a in [(n, inputs[n]) for n in _INS] + [("cos", cos_t), ("sin", sin_t)]:
        arrays[f"in_{name}"] = np.ascontiguousarray(a)
        args.append(nc.dram_tensor(f"in_{name}", arrays[f"in_{name}"].shape, F32, kind="ExternalInput").ap())
    args.append(nc.dram_tensor("out", (1, S, D), F32, kind="ExternalOutput").ap())
    build(nc, *args)
    r = run_bass_kernel_spmd(nc, [arrays], core_ids=[0])
    return r.results[0]["out"]
```
